# Optimizing a Trainium2 kernel written in Bass

```python
import jax, jax.numpy as jnp
from jax import lax
import numpy as np
import jax
import jax.numpy as jnp

D_MODEL = 1024
BATCH = 1
SEQ = 256
DEPTH = 2

HEAD_DIM = 64
D_RNN = D_MODEL // 2
H_RNN = D_RNN // HEAD_DIM
RNN_BLOCK = D_RNN // H_RNN
CONV_W = 4
RG_C = 8.0
H_FOX = (D_MODEL // 2) // HEAD_DIM
FOX_W = H_FOX * HEAD_DIM
H_SB = D_MODEL // HEAD_DIM
SB_W = H_SB * HEAD_DIM
D_FF = 11 * D_MODEL // 4
Q_BLOCK = 128
RMS_EPS = 1e-6
N_EVEN = (DEPTH + 1) // 2
N_ODD = DEPTH // 2
HY_IN = 2 * D_RNN + 3 * FOX_W + H_FOX
HY_MIX = D_RNN + FOX_W


def _rmsnorm(x, g):
    x32 = x.astype(jnp.float32)
    y = x32 * lax.rsqrt(jnp.mean(x32 * x32, axis=-1, keepdims=True) + RMS_EPS)
    return (y * g.astype(jnp.float32)).astype(x.dtype)

def _swiglu(h, w_in, w_out):
    a, b = jnp.split(h @ w_in, 2, axis=-1)
    return (jax.nn.silu(a) * b) @ w_out

def _lin_combine(left, right):
    a1, b1 = left
    a2, b2 = right
    return a1 * a2, a2 * b1 + b2

def _rglru_branch(u, gate, conv_w, conv_b, gate_w, gate_b, lam):
    B, S, _ = u.shape
    up = jnp.pad(u, ((0, 0), (CONV_W - 1, 0), (0, 0)))
    xc = conv_b + sum(conv_w[j] * up[:, j:j + S] for j in range(CONV_W))
    xh = xc.reshape(B, S, H_RNN, RNN_BLOCK)
    g = jnp.einsum('bshi,ghij->gbshj', xh, gate_w).reshape(2, B, S, D_RNN) + gate_b[:, None, None, :]
    r = jax.nn.sigmoid(g[0].astype(jnp.float32))
    i = jax.nn.sigmoid(g[1].astype(jnp.float32))
    log_a = -RG_C * r * jax.nn.softplus(-lam.astype(jnp.float32))
    a = jnp.exp(log_a)
    b = jnp.sqrt(-jnp.expm1(2.0 * log_a)) * (i * xc.astype(jnp.float32))
    _, h = lax.associative_scan(_lin_combine, (a, b), axis=1)
    return h.astype(u.dtype) * jax.nn.gelu(gate)

def _to_query_blocks(q):
    B, H, S, d = q.shape
    return q.reshape(B, H, S // Q_BLOCK, Q_BLOCK, d).transpose(2, 0, 1, 3, 4)

def _from_query_blocks(o):
    nb, B, H, QB, d = o.shape
    return o.transpose(1, 0, 3, 2, 4).reshape(B, nb * QB, H * d)

def _fox_attention(q, k, v, logf):
    B, H, S, d = q.shape
    c = jnp.cumsum(logf, axis=-1)
    nb = S // Q_BLOCK
    qb = _to_query_blocks(q)
    cb = c.reshape(B, H, nb, Q_BLOCK).transpose(2, 0, 1, 3)
    kpos = jnp.arange(S)
    scale = d ** -0.5

    def block(args):
        qi, ci, bi = args
        qpos = bi * Q_BLOCK + jnp.arange(Q_BLOCK)
        s = jnp.einsum('bhqd,bhkd->bhqk', qi, k).astype(jnp.float32) * scale
        s = s + ci[..., None] - c[:, :, None, :]
        s = jnp.where(kpos[None, :] <= qpos[:, None], s, -jnp.inf)
        p = jax.nn.softmax(s, axis=-1)
        return jnp.einsum('bhqk,bhkd->bhqd', p.astype(v.dtype), v)

    return _from_query_blocks(lax.map(block, (qb, cb, jnp.arange(nb))))

def _stick_breaking_attention(q, k, v):
    B, H, S, d = q.shape
    nb = S // Q_BLOCK
    qb = _to_query_blocks(q)
    kpos = jnp.arange(S)
    scale = d ** -0.5

    def block(args):
        qi, bi = args
        qpos = bi * Q_BLOCK + jnp.arange(Q_BLOCK)
        mask = kpos[None, :] < qpos[:, None]
        z = jnp.einsum('bhqd,bhkd->bhqk', qi, k).astype(jnp.float32) * scale
        log_nb = jnp.where(mask, jax.nn.log_sigmoid(-z), 0.0)
        after = lax.cumsum(log_nb, axis=3, reverse=True) - log_nb
        w = jnp.where(mask, jnp.exp(jax.nn.log_sigmoid(z) + after), 0.0)
        return jnp.einsum('bhqk,bhkd->bhqd', w.astype(v.dtype), v)

    return _from_query_blocks(lax.map(block, (qb, jnp.arange(nb))))

def _heads(t, n):
    B, S, _ = t.shape
    return t.reshape(B, S, n, HEAD_DIM)

def _hybrid_mixer(h, w_in, conv_w, conv_b, gate_w, gate_b, lam, f_b, qk_g, w_out):
    proj = h @ w_in
    o = 2 * D_RNN
    u, gate, q, k, v, f = jnp.split(proj, [D_RNN, o, o + FOX_W, o + 2 * FOX_W, o + 3 * FOX_W], axis=-1)
    y_rnn = _rglru_branch(u, gate, conv_w, conv_b, gate_w, gate_b, lam)
    qh = _rmsnorm(_heads(q, H_FOX), qk_g[0]).transpose(0, 2, 1, 3)
    kh = _rmsnorm(_heads(k, H_FOX), qk_g[1]).transpose(0, 2, 1, 3)
    vh = _heads(v, H_FOX).transpose(0, 2, 1, 3)
    logf = jax.nn.log_sigmoid((f + f_b).astype(jnp.float32)).transpose(0, 2, 1)
    y_fox = _fox_attention(qh, kh, vh, logf)
    return jnp.concatenate([y_rnn, y_fox], axis=-1) @ w_out

def _sb_mixer(h, w_qkv, w_out):
    q, k, v = jnp.split(h @ w_qkv, 3, axis=-1)
    qh, kh, vh = (_heads(t, H_SB).transpose(0, 2, 1, 3) for t in (q, k, v))
    return _stick_breaking_attention(qh, kh, vh) @ w_out

def first_inputs(seed: int = 0) -> dict:
    key = jax.random.key(seed)
    ks = jax.random.split(key, 20)
    f32 = jnp.float32

    def nrm(k, shape, fan_in):
        return jax.random.normal(k, shape, f32) * (fan_in ** -0.5)

    a0 = jax.random.uniform(ks[9], (N_EVEN, D_RNN), f32, 0.9, 0.999)
    return {
        "x": jax.random.normal(ks[0], (BATCH, SEQ, D_MODEL), f32),
        "ffn_norm": 1.0 + 0.05 * jax.random.normal(ks[1], (DEPTH, 2, D_MODEL), f32),
        "ffn_w_in": nrm(ks[2], (DEPTH, 2, D_MODEL, 2 * D_FF), D_MODEL),
        "ffn_w_out": nrm(ks[3], (DEPTH, 2, D_FF, D_MODEL), D_FF),
        "mix_norm": 1.0 + 0.05 * jax.random.normal(ks[4], (DEPTH, D_MODEL), f32),
        "hy_w_in": nrm(ks[5], (N_EVEN, D_MODEL, HY_IN), D_MODEL),
        "rg_conv_w": nrm(ks[6], (N_EVEN, CONV_W, D_RNN), CONV_W),
        "rg_conv_b": 0.02 * jax.random.normal(ks[7], (N_EVEN, D_RNN), f32),
        "rg_gate_w": nrm(ks[8], (N_EVEN, 2, H_RNN, RNN_BLOCK, RNN_BLOCK), RNN_BLOCK),
        "rg_gate_b": 0.02 * jax.random.normal(ks[10], (N_EVEN, 2, D_RNN), f32),
        "rg_lambda": jnp.log(a0) - jnp.log1p(-a0),
        "fox_fgate_b": jax.random.uniform(ks[11], (N_EVEN, H_FOX), f32, 1.0, 4.0),
        "fox_qk_norm": 1.0 + 0.05 * jax.random.normal(ks[12], (N_EVEN, 2, HEAD_DIM), f32),
        "hy_w_out": nrm(ks[13], (N_EVEN, HY_MIX, D_MODEL), HY_MIX),
        "sb_w_qkv": nrm(ks[14], (N_ODD, D_MODEL, 3 * SB_W), D_MODEL),
        "sb_w_out": nrm(ks[15], (N_ODD, SB_W, D_MODEL), SB_W),
    }

def first_block(x, ffn_norm, ffn_w_in, ffn_w_out, mix_norm, hy_w_in, rg_conv_w, rg_conv_b,
              rg_gate_w, rg_gate_b, rg_lambda, fox_fgate_b, fox_qk_norm, hy_w_out,
              sb_w_qkv, sb_w_out):
    for layer in range(DEPTH):
        x = x + 0.5 * _swiglu(_rmsnorm(x, ffn_norm[layer, 0]), ffn_w_in[layer, 0], ffn_w_out[layer, 0])
        h = _rmsnorm(x, mix_norm[layer])
        if layer % 2 == 0:
            e = layer // 2
            y = _hybrid_mixer(h, hy_w_in[e], rg_conv_w[e], rg_conv_b[e], rg_gate_w[e], rg_gate_b[e],
                              rg_lambda[e], fox_fgate_b[e], fox_qk_norm[e], hy_w_out[e])
        else:
            o = layer // 2
            y = _sb_mixer(h, sb_w_qkv[o], sb_w_out[o])
        x = x + y
        x = x + 0.5 * _swiglu(_rmsnorm(x, ffn_norm[layer, 1]), ffn_w_in[layer, 1], ffn_w_out[layer, 1])
    return x


GRID_W = 64
CTX_LEN = 256
A_HEADS = 8
A_KV_HEADS = 2
A_WINDOW = 128
A_BLOCK = 128
B_HEADS = 8
NA_ROWS = 8
NA_COLS = 16
QA_W = A_HEADS * HEAD_DIM
KVA_W = A_KV_HEADS * HEAD_DIM
QKVB_W = B_HEADS * HEAD_DIM
EVEN_SPLITS = (QA_W, QA_W + KVA_W, QA_W + 2 * KVA_W, QA_W + 2 * KVA_W + QKVB_W, QA_W + 2 * KVA_W + 2 * QKVB_W)
EVEN_IN = QA_W + 2 * KVA_W + 3 * QKVB_W
EVEN_OUT = (A_HEADS + B_HEADS) * HEAD_DIM
C_HEADS = 16
C_Q_RANK = 384
C_KV_RANK = 256
C_NOPE = 64
C_ROPE = 32
C_V = 64
C_IN = C_Q_RANK + C_KV_RANK + C_ROPE
C_OUT = C_HEADS * C_V
D_FF_2 = 4 * D_MODEL
N_EVEN_2 = (DEPTH + 1) // 2
N_ODD_2 = DEPTH // 2
ROPE_THETA = 10000.0
NORM_EPS = 1e-6
NEG_INF = -1e30


def rms_norm(x, g):
    xf = x.astype(jnp.float32)
    y = xf * lax.rsqrt(jnp.mean(xf * xf, axis=-1, keepdims=True) + NORM_EPS)
    return (y * g.astype(jnp.float32)).astype(x.dtype)

def modulate(h, shift, scale):
    return h * (1 + scale) + shift

def adaln(cond, w, b):
    m = jax.nn.silu(cond) @ w + b
    return jnp.split(m[:, None, :], 6, axis=-1)

def rope_1d(x, pos):
    half = x.shape[-1] // 2
    inv = ROPE_THETA ** (-jnp.arange(half, dtype=jnp.float32) / half)
    ang = pos.astype(jnp.float32)[:, None] * inv[None, :]
    cos, sin = jnp.cos(ang)[:, None, :], jnp.sin(ang)[:, None, :]
    x1, x2 = x[..., :half], x[..., half:]
    return jnp.concatenate([x1 * cos - x2 * sin, x1 * sin + x2 * cos], axis=-1).astype(x.dtype)

def rope_2d(x, row, col):
    half = x.shape[-1] // 2
    return jnp.concatenate([rope_1d(x[..., :half], row), rope_1d(x[..., half:], col)], axis=-1)

def squared_relu_mlp(h, w1, w2):
    return jnp.square(jax.nn.relu(h @ w1)) @ w2

def ctx_self_attention(q, k, v, scale, sink=None):
    bsz, n, hq, dq = q.shape
    g = k.shape[2]
    r = hq // g
    qg = q.reshape(bsz, n, g, r, dq)
    s = jnp.einsum('bqgrd,bkgd->bgrqk', qg, k, preferred_element_type=jnp.float32) * scale
    if sink is not None:
        sk = jnp.broadcast_to(sink.astype(jnp.float32).reshape(g, r)[None, :, :, None, None], (bsz, g, r, n, 1))
        s = jnp.concatenate([s, sk], axis=-1)
    p = jax.nn.softmax(s, axis=-1)[..., :n].astype(v.dtype)
    o = jnp.einsum('bgrqk,bkgd->bqgrd', p, v)
    return o.reshape(bsz, n, hq * v.shape[-1])

def window_attention(q, k, v, kc, vc, sink):
    bsz, seq, hq, d = q.shape
    g = k.shape[2]
    r = hq // g
    nb = seq // A_BLOCK
    qb = q.reshape(bsz, nb, A_BLOCK, g, r, d)

    def band(t):
        tb = jnp.pad(t.reshape(bsz, nb, A_BLOCK, g, d), ((0, 0), (1, 1), (0, 0), (0, 0), (0, 0)))
        return jnp.concatenate([tb[:, :-2], tb[:, 1:-1], tb[:, 2:]], axis=2)

    kb, vb = band(k), band(v)
    qpos = jnp.arange(seq).reshape(nb, A_BLOCK)
    kpos = (jnp.arange(nb)[:, None] - 1) * A_BLOCK + jnp.arange(3 * A_BLOCK)[None, :]
    valid = ((kpos[:, None, :] >= 0) & (kpos[:, None, :] < seq)
             & (jnp.abs(qpos[:, :, None] - kpos[:, None, :]) <= A_WINDOW))
    scale = d ** -0.5
    s_loc = jnp.einsum('bnqgrd,bnkgd->bngrqk', qb, kb, preferred_element_type=jnp.float32) * scale
    s_loc = jnp.where(valid[None, :, None, None], s_loc, NEG_INF)
    s_ctx = jnp.einsum('bnqgrd,bcgd->bngrqc', qb, kc, preferred_element_type=jnp.float32) * scale
    s_sink = jnp.broadcast_to(sink.astype(jnp.float32).reshape(g, r)[None, None, :, :, None, None],
                              (bsz, nb, g, r, A_BLOCK, 1))
    p = jax.nn.softmax(jnp.concatenate([s_loc, s_ctx, s_sink], axis=-1), axis=-1).astype(v.dtype)
    nloc = 3 * A_BLOCK
    nctx = kc.shape[1]
    o = (jnp.einsum('bngrqk,bnkgd->bnqgrd', p[..., :nloc], vb)
         + jnp.einsum('bngrqc,bcgd->bnqgrd', p[..., nloc:nloc + nctx], vc))
    return o.reshape(bsz, seq, hq * d)

def neighbourhood_attention(q, k, v, kc, vc, rpb, rows_n):
    bsz, _, h, d = q.shape
    kh = min(NA_ROWS, rows_n)
    r = jnp.arange(rows_n)
    row_idx = jnp.clip(r - kh // 2, 0, rows_n - kh)[:, None] + jnp.arange(kh)[None, :]
    cq = jnp.arange(GRID_W)
    c0 = jnp.clip(cq - NA_COLS // 2, 0, GRID_W - NA_COLS)
    col_ok = (cq[None, :] >= c0[:, None]) & (cq[None, :] < c0[:, None] + NA_COLS)
    dri = row_idx - r[:, None] + NA_ROWS - 1
    dci = jnp.clip(cq[None, :] - cq[:, None], 1 - NA_COLS, NA_COLS - 1) + NA_COLS - 1
    bias = rpb.astype(jnp.float32)[:, dri[:, None, :, None], dci[None, :, None, :]]
    bias = jnp.moveaxis(bias, 0, 1)
    qg = q.reshape(bsz, rows_n, GRID_W, h, d)
    kg = k.reshape(bsz, rows_n, GRID_W, h, d)[:, row_idx]
    vg = v.reshape(bsz, rows_n, GRID_W, h, d)[:, row_idx]
    scale = d ** -0.5
    s_loc = jnp.einsum('brqhd,brikhd->brhqik', qg, kg, preferred_element_type=jnp.float32) * scale + bias[None]
    s_loc = jnp.where(col_ok[:, None, :], s_loc, NEG_INF).reshape(bsz, rows_n, h, GRID_W, kh * GRID_W)
    s_ctx = jnp.einsum('brqhd,bchd->brhqc', qg, kc, preferred_element_type=jnp.float32) * scale
    p = jax.nn.softmax(jnp.concatenate([s_loc, s_ctx], axis=-1), axis=-1).astype(v.dtype)
    nloc = kh * GRID_W
    p_loc = p[..., :nloc].reshape(bsz, rows_n, h, GRID_W, kh, GRID_W)
    o = jnp.einsum('brhqik,brikhd->brqhd', p_loc, vg) + jnp.einsum('brhqc,bchd->brqhd', p[..., nloc:], vc)
    return o.reshape(bsz, rows_n * GRID_W, h * d)

def blockwise_dense_attention(q, k, v, kc, vc, scale):
    bsz, seq, h, dq = q.shape
    nb = seq // Q_BLOCK
    kall = jnp.concatenate([kc, k], axis=1)
    vall = jnp.concatenate([vc, v], axis=1)
    qb = jnp.moveaxis(q.reshape(bsz, nb, Q_BLOCK, h, dq), 1, 0)

    def one_block(qblk):
        s = jnp.einsum('bqhd,bkhd->bhqk', qblk, kall, preferred_element_type=jnp.float32) * scale
        p = jax.nn.softmax(s, axis=-1).astype(vall.dtype)
        return jnp.einsum('bhqk,bkhd->bqhd', p, vall)

    o = lax.map(one_block, qb)
    return jnp.moveaxis(o, 0, 1).reshape(bsz, seq, h * v.shape[-1])

def even_mixer(h_lat, h_ctx, row, col, rows_n, w_in, w_out, a_qn, a_kn, a_sink, b_qn, b_kn, b_rpb, need_ctx_out):
    def heads(hh):
        bsz, n, _ = hh.shape
        qa, ka, va, qb, kb, vb = jnp.split(hh @ w_in, EVEN_SPLITS, axis=-1)
        qa = rms_norm(qa.reshape(bsz, n, A_HEADS, HEAD_DIM), a_qn)
        ka = rms_norm(ka.reshape(bsz, n, A_KV_HEADS, HEAD_DIM), a_kn)
        va = va.reshape(bsz, n, A_KV_HEADS, HEAD_DIM)
        qb = rms_norm(qb.reshape(bsz, n, B_HEADS, HEAD_DIM), b_qn)
        kb = rms_norm(kb.reshape(bsz, n, B_HEADS, HEAD_DIM), b_kn)
        vb = vb.reshape(bsz, n, B_HEADS, HEAD_DIM)
        return qa, ka, va, qb, kb, vb

    qa, ka, va, qb, kb, vb = heads(h_lat)
    qa_c, ka_c, va_c, qb_c, kb_c, vb_c = heads(h_ctx)
    qa = rope_2d(qa, row, col)
    ka = rope_2d(ka, row, col)
    o_a = window_attention(qa, ka, va, ka_c, va_c, a_sink)
    o_b = neighbourhood_attention(qb, kb, vb, kb_c, vb_c, b_rpb, rows_n)
    y_lat = jnp.concatenate([o_a, o_b], axis=-1) @ w_out
    y_ctx = None
    if need_ctx_out:
        scale = HEAD_DIM ** -0.5
        oa_c = ctx_self_attention(qa_c, ka_c, va_c, scale, a_sink)
        ob_c = ctx_self_attention(qb_c, kb_c, vb_c, scale)
        y_ctx = jnp.concatenate([oa_c, ob_c], axis=-1) @ w_out
    return y_lat, y_ctx

def mla_project(hh, w_in, qa_norm, kva_norm, w_uq, w_ukv, qn_nope, qn_rope, kn_nope, kn_rope):
    bsz, n, _ = hh.shape
    cq, ckv, kr = jnp.split(hh @ w_in, (C_Q_RANK, C_Q_RANK + C_KV_RANK), axis=-1)
    q = (rms_norm(cq, qa_norm) @ w_uq).reshape(bsz, n, C_HEADS, C_NOPE + C_ROPE)
    kv = (rms_norm(ckv, kva_norm) @ w_ukv).reshape(bsz, n, C_HEADS, C_NOPE + C_V)
    q_nope = rms_norm(q[..., :C_NOPE], qn_nope)
    q_rope = rms_norm(q[..., C_NOPE:], qn_rope)
    k_nope = rms_norm(kv[..., :C_NOPE], kn_nope)
    v = kv[..., C_NOPE:]
    k_rope = rms_norm(kr[:, :, None, :], kn_rope)
    return q_nope, q_rope, k_nope, k_rope, v

def odd_mixer(h_lat, h_ctx, row, col, w_in, qa_norm, kva_norm, w_uq, w_ukv,
              qn_nope, qn_rope, kn_nope, kn_rope, w_out, need_ctx_out):
    q_nope, q_rope, k_nope, k_rope, v = mla_project(h_lat, w_in, qa_norm, kva_norm, w_uq, w_ukv,
                                                    qn_nope, qn_rope, kn_nope, kn_rope)
    q = jnp.concatenate([q_nope, rope_2d(q_rope, row, col)], axis=-1)
    k_rope = rope_2d(k_rope, row, col)
    k = jnp.concatenate([k_nope, jnp.broadcast_to(k_rope, k_nope.shape[:-1] + (C_ROPE,))], axis=-1)
    qc_nope, qc_rope, kc_nope, kc_rope, vc = mla_project(h_ctx, w_in, qa_norm, kva_norm, w_uq, w_ukv,
                                                         qn_nope, qn_rope, kn_nope, kn_rope)
    kc = jnp.concatenate([kc_nope, jnp.broadcast_to(kc_rope, kc_nope.shape[:-1] + (C_ROPE,))], axis=-1)
    scale = (C_NOPE + C_ROPE) ** -0.5
    y_lat = blockwise_dense_attention(q, k, v, kc, vc, scale) @ w_out
    y_ctx = None
    if need_ctx_out:
        qc = jnp.concatenate([qc_nope, qc_rope], axis=-1)
        y_ctx = ctx_self_attention(qc, kc, vc, scale) @ w_out
    return y_lat, y_ctx

def second_inputs(seed: int = 0) -> dict:
    key = jax.random.key(seed)
    ks = jax.random.split(key, 32)
    f32 = jnp.float32

    def nrm(k, shape, fan_in):
        return jax.random.normal(k, shape, f32) * fan_in ** -0.5

    def gain(k, shape):
        return 1.0 + 0.05 * jax.random.normal(k, shape, f32)

    return {
        'x': jax.random.normal(ks[0], (BATCH, SEQ, D_MODEL), f32),
        'c': jax.random.normal(ks[1], (BATCH, D_MODEL), f32),
        'ctx': jax.random.normal(ks[2], (BATCH, CTX_LEN, D_MODEL), f32),
        'c_ctx': jax.random.normal(ks[3], (D_MODEL,), f32),
        'ada_w': nrm(ks[4], (DEPTH, D_MODEL, 6 * D_MODEL), D_MODEL),
        'ada_b': 0.02 * jax.random.normal(ks[5], (DEPTH, 6 * D_MODEL), f32),
        'norm_mix': gain(ks[6], (DEPTH, D_MODEL)),
        'norm_mlp': gain(ks[7], (DEPTH, D_MODEL)),
        'mlp_w1': nrm(ks[8], (DEPTH, D_MODEL, D_FF_2), D_MODEL),
        'mlp_w2': nrm(ks[9], (DEPTH, D_FF_2, D_MODEL), D_FF_2),
        'e_w_in': nrm(ks[10], (N_EVEN_2, D_MODEL, EVEN_IN), D_MODEL),
        'e_w_out': nrm(ks[11], (N_EVEN_2, EVEN_OUT, D_MODEL), EVEN_OUT),
        'a_q_norm': gain(ks[12], (N_EVEN_2, HEAD_DIM)),
        'a_k_norm': gain(ks[13], (N_EVEN_2, HEAD_DIM)),
        'a_sink': jax.random.normal(ks[14], (N_EVEN_2, A_HEADS), f32),
        'b_q_norm': gain(ks[15], (N_EVEN_2, HEAD_DIM)),
        'b_k_norm': gain(ks[16], (N_EVEN_2, HEAD_DIM)),
        'b_rpb': 0.1 * jax.random.normal(ks[17], (N_EVEN_2, B_HEADS, 2 * NA_ROWS - 1, 2 * NA_COLS - 1), f32),
        'o_w_in': nrm(ks[18], (N_ODD_2, D_MODEL, C_IN), D_MODEL),
        'o_qa_norm': gain(ks[19], (N_ODD_2, C_Q_RANK)),
        'o_kva_norm': gain(ks[20], (N_ODD_2, C_KV_RANK)),
        'o_w_uq': nrm(ks[21], (N_ODD_2, C_Q_RANK, C_HEADS * (C_NOPE + C_ROPE)), C_Q_RANK),
        'o_w_ukv': nrm(ks[22], (N_ODD_2, C_KV_RANK, C_HEADS * (C_NOPE + C_V)), C_KV_RANK),
        'o_qn_nope': gain(ks[23], (N_ODD_2, C_NOPE)),
        'o_qn_rope': gain(ks[24], (N_ODD_2, C_ROPE)),
        'o_kn_nope': gain(ks[25], (N_ODD_2, C_NOPE)),
        'o_kn_rope': gain(ks[26], (N_ODD_2, C_ROPE)),
        'o_w_out': nrm(ks[27], (N_ODD_2, C_OUT, D_MODEL), C_OUT),
    }

def second_block(x, c, ctx, c_ctx, ada_w, ada_b, norm_mix, norm_mlp, mlp_w1, mlp_w2,
              e_w_in, e_w_out, a_q_norm, a_k_norm, a_sink, b_q_norm, b_k_norm, b_rpb,
              o_w_in, o_qa_norm, o_kva_norm, o_w_uq, o_w_ukv,
              o_qn_nope, o_qn_rope, o_kn_nope, o_kn_rope, o_w_out):
    seq = x.shape[1]
    rows_n = seq // GRID_W
    t = jnp.arange(seq, dtype=jnp.int32)
    row, col = t // GRID_W, t % GRID_W
    for i in range(DEPTH):
        last = i == DEPTH - 1
        j = i // 2
        sh1, sc1, g1, sh2, sc2, g2 = adaln(c, ada_w[i], ada_b[i])
        csh1, csc1, cg1, csh2, csc2, cg2 = adaln(c_ctx[None, :], ada_w[i], ada_b[i])
        h_lat = modulate(rms_norm(x, norm_mix[i]), sh1, sc1)
        h_ctx = modulate(rms_norm(ctx, norm_mix[i]), csh1, csc1)
        if i % 2 == 0:
            y_lat, y_ctx = even_mixer(h_lat, h_ctx, row, col, rows_n, e_w_in[j], e_w_out[j],
                                      a_q_norm[j], a_k_norm[j], a_sink[j],
                                      b_q_norm[j], b_k_norm[j], b_rpb[j], not last)
        else:
            y_lat, y_ctx = odd_mixer(h_lat, h_ctx, row, col, o_w_in[j], o_qa_norm[j], o_kva_norm[j],
                                     o_w_uq[j], o_w_ukv[j], o_qn_nope[j], o_qn_rope[j],
                                     o_kn_nope[j], o_kn_rope[j], o_w_out[j], not last)
        x = x + g1 * y_lat
        x = x + g2 * squared_relu_mlp(modulate(rms_norm(x, norm_mlp[i]), sh2, sc2), mlp_w1[i], mlp_w2[i])
        if not last:
            ctx = ctx + cg1 * y_ctx
            ctx = ctx + cg2 * squared_relu_mlp(modulate(rms_norm(ctx, norm_mlp[i]), csh2, csc2),
                                               mlp_w1[i], mlp_w2[i])
    return x


def setup_inputs(seed=0):
    out = dict(first_inputs(seed))
    for name, value in second_inputs(seed + 1).items():
        if name != "x":
            out[name + "_2"] = value
    return out


def reference(
    x, ffn_norm, ffn_w_in, ffn_w_out, mix_norm, hy_w_in, rg_conv_w, rg_conv_b, rg_gate_w,
    rg_gate_b, rg_lambda, fox_fgate_b, fox_qk_norm, hy_w_out, sb_w_qkv, sb_w_out, c_2, ctx_2,
    c_ctx_2, ada_w_2, ada_b_2, norm_mix_2, norm_mlp_2, mlp_w1_2, mlp_w2_2, e_w_in_2, e_w_out_2,
    a_q_norm_2, a_k_norm_2, a_sink_2, b_q_norm_2, b_k_norm_2, b_rpb_2, o_w_in_2, o_qa_norm_2,
    o_kva_norm_2, o_w_uq_2, o_w_ukv_2, o_qn_nope_2, o_qn_rope_2, o_kn_nope_2, o_kn_rope_2,
    o_w_out_2,
):
    x = first_block(
        x, ffn_norm, ffn_w_in, ffn_w_out, mix_norm, hy_w_in, rg_conv_w, rg_conv_b, rg_gate_w,
        rg_gate_b, rg_lambda, fox_fgate_b, fox_qk_norm, hy_w_out, sb_w_qkv, sb_w_out,
    )
    return second_block(
        x, c_2, ctx_2, c_ctx_2, ada_w_2, ada_b_2, norm_mix_2, norm_mlp_2, mlp_w1_2, mlp_w2_2,
        e_w_in_2, e_w_out_2, a_q_norm_2, a_k_norm_2, a_sink_2, b_q_norm_2, b_k_norm_2, b_rpb_2,
        o_w_in_2, o_qa_norm_2, o_kva_norm_2, o_w_uq_2, o_w_ukv_2, o_qn_nope_2, o_qn_rope_2,
        o_kn_nope_2, o_kn_rope_2, o_w_out_2,
    )


_drawn_inputs = setup_inputs


def setup_inputs(seed=0):
    import zlib

    import numpy as np

    out = dict(_drawn_inputs(seed))
    spreads = {}
    factors = {'rg_conv_b': 2.921,
     'rg_gate_b': 8.0,
     'fox_qk_norm': 4.707,
     'norm_mix_2': 8.0,
     'a_q_norm_2': 8.0,
     'a_k_norm_2': 8.0,
     'a_sink_2': 8.0,
     'b_q_norm_2': 8.0,
     'b_k_norm_2': 8.0,
     'b_rpb_2': 8.0,
     'o_qa_norm_2': 8.0,
     'o_kva_norm_2': 7.807,
     'o_qn_nope_2': 8.0,
     'o_qn_rope_2': 8.0,
     'o_kn_nope_2': 8.0,
     'o_kn_rope_2': 8.0}
    for name, (base, spread) in spreads.items():
        noise = np.random.default_rng([zlib.crc32(name.encode()), seed]).standard_normal(out[name].shape)
        drawn = base * np.exp(spread * noise) if base else spread * noise
        out[name] = jnp.asarray(drawn.astype(out[name].dtype))
    for name, factor in factors.items():
        out[name] = (out[name] * factor).astype(out[name].dtype)
    return out
```

```python
from contextlib import ExitStack

import numpy as np

import concourse.bass as bass
from concourse import mybir

ALU = mybir.AluOpType
ACT = mybir.ActivationFunctionType
F32 = mybir.dt.float32
F32R = mybir.dt.float32r
AX_X = mybir.AxisListType.X

P = 128
D = 1024
DC = D // P
T = 256
TJ = 2 * T
HD = 64
FF = 2816
FC = FF // P
FH = FC // 2
FF2 = 4096
MC = FF2 // P
EPS = 1e-6
NEG = -1e30
SLOT = 16 * P
MQ, MR = 96, 32
GRID = 64
NA_COLS = 16

_VECS = [("ffn_norm", 32), ("mix_norm", 16), ("conv_w", 16), ("conv_b", 4), ("gate_b", 8), ("lam", 4),
         ("fox_g", 2), ("fox_fb", 1), ("norm_mix", 16), ("norm_mlp", 16), ("a_qn", 1), ("a_kn", 1),
         ("b_qn", 1), ("b_kn", 1), ("qa_norm", 3), ("kva_norm", 2), ("qn", 1), ("kn", 1),
         ("ada_b", 96), ("cond", 16), ("sink", 8)]
VOFF, _n = {}, 0
for _name, _w in _VECS:
    VOFF[_name] = _n
    _n += _w
NV = _n

ADA_PANELS = 48
ADA_BANK = 2


def weight_plan():
    return [("ffn_in0", 22, SLOT), ("ffn_out0", 16, FH * P), ("hy_in", 10, SLOT), ("hy_out", 4, SLOT),
            ("ffn_in1", 22, SLOT), ("ffn_out1", 16, FH * P), ("ffn_in2", 22, SLOT), ("ffn_out2", 16, FH * P),
            ("sb_in", 12, SLOT), ("sb_out", 4, SLOT), ("ffn_in3", 22, SLOT), ("ffn_out3", 16, FH * P),
            ("e_in", 9, SLOT), ("e_out", 4, SLOT),
            ("mlp_in0", 8, SLOT), ("mlp_out0", 8, SLOT), ("mlp_in1", 8, SLOT), ("mlp_out1", 8, SLOT),
            ("o_in", 3, SLOT), ("o_uq", 3, SLOT), ("o_ukv", 2, SLOT), ("o_out", 4, SLOT),
            ("mlp_in2", 16, SLOT), ("mlp_out2", 16, SLOT)]


def build(nc, ap):
    with ExitStack() as ctx:
        def sb(name, shape, dt=F32):
            return ctx.enter_context(nc.sbuf_tensor(name, shape, dt))

        def sem(name):
            return ctx.enter_context(nc.semaphore(name))

        x = sb("x_res", [P, DC, TJ])
        hh = sb("h_hi", [P, DC, TJ], F32R)
        hl = sb("h_lo", [P, DC, TJ], F32R)
        raw = [sb(f"raw{i}", [P, SLOT]) for i in range(2)]
        wh = [sb(f"w_hi{i}", [P, SLOT], F32R) for i in range(2)]
        wl = [sb(f"w_lo{i}", [P, SLOT], F32R) for i in range(2)]
        scr = sb("scratch", [P, 4096])
        small = sb("small", [P, 64])
        vecs = sb("vecs", [P, NV])
        base_c = sb("base_c", [P, 2 * P])
        mods = sb("mods", [P, 96, 2])
        gmod = sb("gmod", [P, 6, DC])
        cond_s = sb("cond_silu", [P, DC, 2])
        raw_a = sb("raw_ada", [P, SLOT])
        creg = sb("const_region", [P, 2720])
        ARENA = 4 * 16384
        at = int(nc.sbuf_usable_end) // 64 * 64 - ARENA - 64
        gh = nc.alloc_sbuf_tensor_at("g_hi", [P, 8192], F32R, offset=at)
        gl = nc.alloc_sbuf_tensor_at("g_lo", [P, 8192], F32R, offset=at + ARENA // 2)
        arena = nc.alloc_sbuf_tensor_at("arena", [P, 16384], F32, offset=at)
        assert int(nc.sbuf_base) <= at

        psum = ctx.enter_context(nc.psum_tensor("psum", [P, 8, 512], F32))
        ident, mean_w = base_c[:, 0:P], base_c[:, P:2 * P]

        class Carve:

            def __init__(self, tile):
                self.tile, self.n = tile, 0

            def __call__(self, *dims):
                w = 1
                for d in dims:
                    w *= d
                v = self.tile[:, self.n:self.n + w]
                self.n += w
                if len(dims) == 2:
                    v = v.rearrange("p (a b) -> p a b", a=dims[0])
                if len(dims) == 3:
                    v = v.rearrange("p (a b c) -> p a b c", a=dims[0], b=dims[1])
                return v

        cs = Carve(scr)
        s_buf, p_buf, pt_buf = cs(2, 512), cs(3, 512), cs(2, 512)
        row_t = cs(512)
        cs2 = Carve(scr)
        sq_buf, tmp_buf = cs2(2, 512), cs2(4, 256)
        ffn_t, ffn_u, ffn_g = cs2(2, 256), cs2(256), cs2(256)
        cs3 = Carve(scr)
        mlp_r, mlp_g = cs3(512), cs3(512)
        cs4 = Carve(scr)
        sb_z, sb_e, sb_n, sb_w = cs4(4, 384), cs4(2, 384), cs4(2, 384), cs4(2, 384)

        ch_ = Carve(arena)
        f_qk, f_v, u_pad, gate_t = ch_(8, T), ch_(2, 512), ch_(4, 260), ch_(4, T)
        xc, ra, ia, th = ch_(4, T), ch_(4, T), ch_(4, T), ch_(4, T)
        fc0 = ch_.n
        f_mask, f_sel, f_bsel, f_eh, gw, wf = ch_(2, T), ch_(8, 16), ch_(8, P), ch_(8, P), ch_(2, 4, P), ch_(8, 8)
        fc1 = ch_.n
        lf, ones_r, ci, cj = ch_(2, T), ch_(T), ch_(2, 8), ch_(8, T)
        assert ch_.n <= 16384
        cb = Carve(arena)
        s_qk, s_v = cb(16, T), cb(2, 1024)
        sc0 = cb.n
        s_mask, s_tri, s_ones = cb(384), cb(P), cb(P)
        sc1 = cb.n
        ca = Carve(arena)
        e_qk, k_dup, a_v, b_v = ca(13, TJ), ca(2, TJ), ca(4, P), ca(4, 512)
        b_bias = ca(2, 8, T)
        ac0 = ca.n
        w_mask, col_mask = ca(2, T), ca(T)
        ac1 = ca.n
        assert ca.n <= 16384
        cc = Carve(creg)
        e_sel, e_bsel, cos_a, sin_a, rot_a = cc(13, 32), cc(13, P), cc(T), cc(T), cc(P)
        NCE = cc.n
        cm = Carve(arena)
        m_q, m_k, m_v = cm(16, T), cm(16, TJ), cm(4, 1024)
        cd = Carve(creg)
        m_sel, m_bsel, cos_m, sin_m, rot_m = cd(16, 32), cd(16, MQ), cd(T), cd(T), cd(MR)
        NCM = cd.n
        cl5 = Carve(arena)
        lat_c, lat_kv = cl5(3, T), cl5(2, TJ)

        def vec(name, i=0, rows=P):
            return vecs[0:rows, VOFF[name] + i:VOFF[name] + i + 1]

        base_loaded = sem("base_loaded")
        phase_loaded = [sem(f"phase_loaded{i}") for i in range(4)]
        bias_loaded = sem("bias_loaded")
        raw_loaded = [sem("raw_loaded0"), sem("raw_loaded1")]
        ada_loaded = sem("ada_loaded")
        ada_done = sem("ada_done")
        ada_in = sem("ada_in")
        hi_ready = sem("hi_ready")
        lo_ready = sem("lo_ready")
        gemm_done = sem("gemm_done")
        bank_free = sem("bank_free")
        tanh_done = sem("tanh_done")
        ffn_seq = sem("ffn_seq")
        g_ready = sem("g_ready")
        h_ready = sem("h_ready")
        seq = sem("seq")
        to_act, from_act = sem("to_act"), sem("from_act")
        to_pe = sem("to_pe")
        sq_ready, sq_used = sem("sq_ready"), sem("sq_used")
        small_done, small_free = sem("small_done"), sem("small_free")
        score_done, score_in = sem("score_done"), sem("score_in")
        exp_done, prob_ready = sem("exp_done"), sem("prob_ready")
        turn_done, turn_in = sem("turn_done"), sem("turn_in")
        pv_done, y_ready = sem("pv_done"), sem("y_ready")
        sb_z_done, sb_z_in, sb_e_done, sb_n_in = sem("sb_z_done"), sem("sb_z_in"), sem("sb_e_done"), sem("sb_n_in")
        sb_i_done, sb_i_in, sb_w_done, sb_o_done, sb_y = (sem("sb_i_done"), sem("sb_i_in"), sem("sb_w_done"),
                                                          sem("sb_o_done"), sem("sb_y"))
        krope_done = sem("krope_done")
        stored = sem("stored")

        def wait(eng, s, v):
            if isinstance(v, int) and v <= 0:
                return
            eng.wait_ge(s, v)

        def loop(eng, n, body, peel):
            if peel:
                body(0)
            if n > peel:
                with eng.Fori(int(peel), n) as i:
                    body(i)

        def pick(t, i, cols):
            if isinstance(i, int):
                return t[:, i, cols]
            return t[:, bass.ds(i, 1), cols].rearrange("p a b -> p (a b)")

        def flat(t, start, size):
            return t[:, start:start + size] if isinstance(start, int) else t[:, bass.ds(start, size)]

        class Pos:

            def __init__(self):
                self.p = self.e = self.u = 0
                self.k = {}

            def n(self, name, by=0):
                self.k[name] = self.k.get(name, 0) + by
                return self.k[name]

        LAST_PANEL = sum(n for _, n, _ in weight_plan()) - 1

        def fox_jobs():
            for h in range(8):
                r = slice(64 * (h % 2), 64 * (h % 2) + 64)
                for t in range(2):
                    yield dict(q=f_qk[r, h // 2, t * P:(t + 1) * P], k=f_qk[r, 4 + h // 2, :], L=T,
                               scale=HD ** -0.5, fox=(h, t), sink=None, bias=None,
                               v=[f_v[:, b, h * HD:(h + 1) * HD] for b in range(2)], y=(4 + h // 2, 0), h=h, t=t)

        def even_jobs():
            for base in (0, T):
                for kind in "ab":
                    for h in range(8):
                        r = slice(64 * (h % 2), 64 * (h % 2) + 64)
                        c = h // 2
                        L = TJ if base == 0 else T
                        k0 = TJ - L
                        tiles = range(k0 // P, 4)
                        for t in range(2):
                            cols = slice(base + t * P, base + (t + 1) * P)
                            if kind == "a":
                                g = h // 4
                                yield dict(q=e_qk[r, c, cols], k=k_dup[r, g, k0:TJ], L=L, scale=HD ** -0.5,
                                           bias=w_mask[:, t, :] if base == 0 else None, fox=None,
                                           sink=vecs[:, VOFF["sink"] + h:VOFF["sink"] + h + 1],
                                           v=[a_v[:, b, g * HD:(g + 1) * HD] for b in tiles], y=(c, base), h=h, t=t)
                            else:
                                yield dict(q=e_qk[r, 5 + c, cols], k=e_qk[r, 9 + c, k0:TJ], L=L, scale=HD ** -0.5,
                                           bias=b_bias[:, t, h, :] if base == 0 else None, fox=None, sink=None,
                                           v=[b_v[:, b, h * HD:(h + 1) * HD] for b in tiles], y=(4 + c, base),
                                           h=h, t=t)

        def latent_jobs():
            for h in range(16):
                for t in range(2):
                    yield dict(q=m_q[0:MQ, h, t * P:(t + 1) * P], k=m_k[0:MQ, h, :], L=TJ, scale=MQ ** -0.5,
                               bias=None, fox=None, sink=None,
                               v=[m_v[:, b, h * HD:(h + 1) * HD] for b in range(4)], y=(h // 2, 0), h=h, t=t)

        block = ctx.enter_context(nc.Block())

        @block.sync
        def _(sp):
            sp.dma_start(vecs[:], ap["vecs"]).then_inc(base_loaded, 16)
            sp.dma_start(x[:], ap["x"]).then_inc(base_loaded, 16)
            sp.dma_start(base_c[:], ap["base_c"]).then_inc(base_loaded, 16)
            p, off = 0, 0
            for name, n, width in weight_plan():
                panels = ap["weights"][off:off + n * P * width].rearrange("(n p w) -> n p w", p=P, w=width)

                def load(j, s, base=p, panels=panels, width=width):
                    wait(sp, lo_ready, 2 * (base + j - 1))
                    src = panels[j] if isinstance(j, int) else panels[bass.ds(j, 1)].rearrange("n p w -> (n p) w")
                    sp.dma_start(raw[s][:, 0:width], src).then_inc(raw_loaded[s], 16)

                first = 2 if p == 0 else 0
                for j in range(first):
                    load(j, (p + j) % 2)
                pairs = (n - first) // 2

                def body(i, base=p, first=first, load=load):
                    for j in range(2):
                        load(2 * i + first + j, (base + j) % 2)
                loop(sp, pairs, body, 0)
                if n % 2:
                    load(n - 1, (p + n - 1) % 2)
                p, off = p + n, off + n * P * width
            wait(sp, bank_free, FINAL_UNITS + 2)
            sp.dma_start(ap["out"], x[:, :, 0:T]).then_inc(stored, 16)
            sp.wait_ge(stored, 16)

        @block.gpsimd
        def _(pool):
            def ada_load(k):
                wait(pool, ada_done, k)
                src = ap["ada"][k] if isinstance(k, int) else ap["ada"][bass.ds(k, 1)].rearrange("n p w -> (n p) w")
                pool.dma_start(raw_a[:], src).then_inc(ada_loaded, 16)

            def ada_loads(first, end):
                if first == 0:
                    ada_load(0)
                with pool.Fori(max(first, 1), end) as k:
                    ada_load(k)

            ada_loads(0, 12)
            pool.wait_ge(gemm_done, EV["hy_in"])
            pool.dma_start(arena[:, fc0:fc1], ap["fox_c"]).then_inc(phase_loaded[0], 16)
            ada_loads(12, 34)
            pool.wait_ge(gemm_done, EV["sb_in"])
            pool.dma_start(arena[:, sc0:sc1], ap["sb_c"]).then_inc(phase_loaded[1], 16)
            pool.dma_start(creg[:, 0:NCE], ap["even_c"]).then_inc(phase_loaded[2], 16)
            ada_loads(34, ADA_PANELS)
            pool.wait_ge(gemm_done, EV["e_in"])
            pool.dma_start(arena[:, ac0:ac1], ap["even_m"]).then_inc(phase_loaded[2], 16)
            pool.dma_start(b_bias.rearrange("p a b c -> p (a b c)"), ap["rpb"]).then_inc(bias_loaded, 16)
            pool.wait_ge(y_ready, Y_EVEN)
            pool.dma_start(creg[:, 0:NCM], ap["latent_c"]).then_inc(phase_loaded[3], 16)

        @block.scalar
        def _(act):
            pos = Pos()

            def hi(s, turn, e, w):
                act.wait_ge(raw_loaded[s], 16 * turn)
                wait(act, gemm_done, e)
                for a in (slice(0, w // 2), slice(w // 2, w)):
                    nc.scalar.activation(wh[s][:, a], raw[s][:, a], ACT.Copy).then_inc(hi_ready, 1)

            def hi_next(rel, i, per_iter, e, w):
                base = pos.p + rel + 1
                if not isinstance(i, int) or base + per_iter * i <= LAST_PANEL:
                    hi(base % 2, base // 2 + i * (per_iter // 2) + 1, e, w)

            def stage(n, per_iter, ev, units, extra=None, peel=0, last=False, w=SLOT):
                def body(i, last_turn=False):
                    for j in range(per_iter):
                        at_end = last_turn and j == per_iter - 1
                        if not (at_end and last):
                            hi_next(j, i, per_iter, pos.e + ev * (per_iter * i + j), SLOT if at_end else w)
                        if extra:
                            extra(i, j)
                if last or w < SLOT:
                    loop(act, n - 1, body, peel)
                    body(n - 1, True)
                else:
                    loop(act, n, body, peel)
                pos.p += n * per_iter
                pos.e += ev * n * per_iter
                pos.u += units * n

            def swiglu(i, j):
                act.wait_ge(gemm_done, pos.e + 2 * i + j + 1)
                nc.scalar.activation(ffn_t[:, j, :], psum[:, (pos.u + j) % 2, 0:T], ACT.Tanh,
                                     scale=0.5).then_inc(tanh_done, 1)

            def ask(func, out, in_, **kw):
                act.wait_ge(to_act, pos.n("ask", 1))
                nc.scalar.activation(out, in_, func, **kw).then_inc(from_act, 1)

            def norm(n):
                ask(ACT.Sqrt, row_t[:, 0:n], row_t[:, 0:n])

            def softmax_jobs(jobs):
                base = pos.n("jobs")
                for k in range(len(jobs) + 2):
                    if k < len(jobs):
                        j, job = base + k, jobs[k]
                        L = job["L"]
                        act.wait_ge(score_in, j + 1)
                        wait(act, turn_done, j - 2)
                        src = s_buf[:, j % 2, 0:L] if job["bias"] is not None or job["fox"] else psum[:, 2 + j % 2, 0:L]
                        sc = 1.0 if job["bias"] is not None or job["fox"] else job["scale"]
                        if job["sink"] is not None:
                            nc.scalar.activation(small[:, 20 + j % 2:21 + j % 2], job["sink"], ACT.Exp,
                                                 bias=small[:, 4 + j % 2:5 + j % 2])
                        nc.scalar.activation(p_buf[:, j % 3, 0:L], src, ACT.Exp, bias=small[:, 4 + j % 2:5 + j % 2],
                                             scale=sc, accum_out=small[:, 8 + j % 2:9 + j % 2]).then_inc(exp_done, 1)
                    if k >= 2:
                        j, job = base + k - 2, jobs[k - 2]
                        L = job["L"]
                        act.wait_ge(turn_done, j + 1)
                        wait(act, pv_done, j - 1)
                        nc.scalar.activation(pt_buf[:, j % 2, 0:L], psum[:, 4 + j % 2, 0:L],
                                             ACT.Copy).then_inc(turn_in, 1)
                pos.n("jobs", len(jobs))

            hi(0, 1, 0, SLOT)
            act.wait_ge(base_loaded, 48)
            cond = vecs[:, VOFF["cond"]:VOFF["cond"] + 16]
            ask(ACT.Tanh, small[:, 24:40], cond, scale=0.5)
            norm(T)
            for f in range(4):
                stage(11, 2, 1, 2, swiglu, peel=int(f == 0))
                stage(4, 4, 1, 2, w=FH * P)
                if f == 0:
                    norm(T)
                    for _ in range(5):
                        stage(1, 2, 1, 2)
                    ask(ACT.Exp, small[:, 44:48], small[:, 44:48])
                    ask(ACT.Ln, small[:, 48:52], small[:, 48:52])
                    for c in range(4):
                        ask(ACT.Tanh, ra[:, c, :], ra[:, c, :], scale=0.5)
                        ask(ACT.Tanh, ia[:, c, :], ia[:, c, :], scale=0.5)
                    ask(ACT.Tanh, th[:, :, :], ra[:, :, :])
                    ask(ACT.Exp, ra[:, :, :], ra[:, :, :])
                    ask(ACT.Sqrt, th[:, :, :], th[:, :, :])
                    ask(ACT.Tanh, ra[:, :, :], xc[:, :, :], scale=0.7978845608028654)
                    ask(ACT.Exp, lf[0:8, 1, :], lf[0:8, 1, :])
                    ask(ACT.Ln, lf[0:8, 1, :], lf[0:8, 1, :], bias=1.0)
                    ask(ACT.Sqrt, row_t[0:16, 0:T], row_t[0:16, 0:T])
                    softmax_jobs(list(fox_jobs()))
                    stage(2, 2, 1, 2)
                    norm(T)
                elif f == 1:
                    norm(T)
                elif f == 2:
                    norm(T)
                    stage(6, 2, 1, 2)
                    nc.scalar.preload_act_table_set("natural_log_exp_and_others")
                    for h in range(16 + 2):
                        if h < 16:
                            b = h % 2
                            act.wait_ge(sb_z_in, h + 1)
                            nc.scalar.activation(sb_e[:, b, :], sb_e[:, b, :], ACT.Exp, scale=-1.0).then_inc(sb_e_done, 1)
                        if h >= 2:
                            g = h - 2
                            act.wait_ge(sb_i_in, g + 1)
                            wait(act, sb_o_done, g - 1)
                            nc.scalar.activation(sb_w[:, g % 2, :], sb_z[:, g % 4, :], ACT.Exp).then_inc(sb_w_done, 1)
                        if h < 16:
                            act.wait_ge(sb_e_done, 2 * h + 1)
                            nc.scalar.activation(sb_e[:, b, :], sb_e[:, b, :], ACT.Ln, bias=1.0).then_inc(sb_e_done, 1)
                    stage(2, 2, 1, 2)
                    norm(T)
            norm(TJ)
            for j in range(9):
                stage(1, 1, 2, 2)
            ask(ACT.Sqrt, row_t[0:26, :], row_t[0:26, :])
            softmax_jobs(list(even_jobs()))
            stage(2, 2, 2, 4)
            norm(TJ)
            for _ in range(2):
                stage(4, 2, 2, 4)
                stage(4, 2, 1, 2)
            norm(TJ)
            for n in (2, 2, 2):
                stage(1, 1, n, n)
            norm(T)
            norm(TJ)
            for n in (3, 3, 2):
                stage(1, 1, n, n)
            for n in (12, 12):
                stage(1, 1, n, n)
            ask(ACT.Sqrt, row_t[0:32, 0:T], row_t[0:32, 0:T])
            ask(ACT.Sqrt, row_t[0:32, :], row_t[0:32, :])
            act.wait_ge(to_act, pos.n("ask", 1))
            for h in range(1, 16):
                nc.scalar.activation(m_k[64:96, h, :], m_k[64:96, 0, :], ACT.Copy).then_inc(krope_done, 1)
            softmax_jobs(list(latent_jobs()))
            stage(2, 2, 1, 2)
            norm(T)
            stage(8, 2, 1, 2)
            stage(4, 4, 1, 2, last=True)

        @block.vector
        def _(dve):
            pos = Pos()
            V = nc.vector

            def do(ins):
                ins.then_inc(seq, 1)
                return pos.n("seq", 1)

            def after(k):
                dve.wait_ge(seq, k)

            def step(ins):
                after(do(ins))

            def ask(ins, extra=None):
                ins.then_inc(to_act, 1)
                dve.wait_ge(from_act, pos.n("ask", 1))

            def tell_pe(ins):
                ins.then_inc(to_pe, 1)
                dve.wait_ge(to_pe, pos.n("to_pe", 1))

            def lo_next(rel, i, per_iter, w=SLOT):
                base = pos.p + rel + 1
                lo(base % 2, base + per_iter * i, w)

            def lo(s, p, w):
                for n, a in enumerate((slice(0, w // 2), slice(w // 2, w))):
                    dve.wait_ge(hi_ready, 2 * p + n + 1)
                    V.tensor_tensor(wl[s][:, a], raw[s][:, a], wh[s][:, a].bitcast(F32),
                                    ALU.subtract).then_inc(lo_ready, 1)

            def stage(n, per_iter, ev, units, evac, peel=0, last=False, w=SLOT):
                def body(i, last_turn=False):
                    for j in range(per_iter):
                        at_end = last_turn and j == per_iter - 1
                        if not (at_end and last):
                            lo_next(j, i, per_iter, SLOT if at_end else w)
                        evac(i, j)
                if last or w < SLOT:
                    loop(dve, n - 1, body, peel)
                    body(n - 1, True)
                else:
                    loop(dve, n, body, peel)
                pos.p += n * per_iter
                pos.e += ev * n * per_iter
                pos.u += units * n

            def freed(u):
                dve.wait_ge(bank_free, u + 3)

            def swiglu_evac():
                base = pos.n("fseq")
                tb, gb, ab = pos.n("tanh"), pos.n("g"), pos.n("ada", 11) - 11

                def evac(i, j):
                    u = pos.u + 2 * i + j
                    bank = (pos.u + j) % 2
                    dve.wait_ge(gemm_done, pos.e + 2 * i + j + 1)
                    dve.wait_ge(tanh_done, tb + 2 * i + j + 1)
                    fs = base + 4 * i + 2 * j
                    V.scalar_tensor_tensor(ffn_u[:], ffn_t[:, j, :], 1.0, psum[:, bank, 0:T], ALU.add,
                                           ALU.mult).then_inc(ffn_seq, 1)
                    dve.wait_ge(ffn_seq, fs + 1)
                    V.tensor_tensor(ffn_g[:], ffn_u[:], psum[:, bank, T:2 * T], ALU.mult).then_inc(bank_free, 1)
                    freed(u)
                    c = 2 * i + j
                    V.tensor_copy(flat(gh, c * T, T), ffn_g[:]).then_inc(ffn_seq, 1)
                    dve.wait_ge(ffn_seq, fs + 2)
                    V.tensor_tensor(flat(gl, c * T, T), ffn_g[:], flat(gh, c * T, T).bitcast(F32),
                                    ALU.subtract).then_inc(g_ready, 1)
                    dve.wait_ge(g_ready, gb + 2 * i + j + 1)
                    if j == 1:
                        ada_evac(ab + i)
                return evac

            def ada_evac(k):
                dve.wait_ge(ada_done, k + 1)
                m = mods[:, 2 * k:2 * k + 2, :] if isinstance(k, int) else mods[:, bass.ds(2 * k, 2), :]
                c0 = VOFF["ada_b"] + 2 * k
                b = vecs[:, c0:c0 + 2] if isinstance(k, int) else vecs[:, bass.ds(c0, 2)]
                V.tensor_tensor(m, psum[:, ADA_BANK, 0:4].rearrange("p (a b) -> p a b", a=2),
                                b.unsqueeze(2).broadcast_to([P, 2, 2]), ALU.add).then_inc(ada_in, 1)

            def residual_evac(factor, per_unit):
                def evac(i, j):
                    if j % per_unit != per_unit - 1:
                        return
                    u = pos.u + 2 * i + j // per_unit
                    bank = (pos.u + j // per_unit) % 2
                    dve.wait_ge(gemm_done, pos.e + 2 * per_unit * i + j + 1)
                    c = 2 * i + j // per_unit
                    V.scalar_tensor_tensor(pick(x, c, slice(0, T)), psum[:, bank, 0:T], factor,
                                           pick(x, c, slice(0, T)), ALU.mult, ALU.add).then_inc(bank_free, 1)
                    freed(u)
                return evac

            def pair_evac(i, j):
                u = pos.u + 2 * i + j
                dve.wait_ge(gemm_done, pos.e + 2 * i + j + 1)
                k = 2 * i + j
                xs = x[:, 2 * k:2 * k + 2, 0:T] if isinstance(k, int) else x[:, bass.ds(2 * k, 2), 0:T]
                V.tensor_tensor(xs, psum[:, (pos.u + j) % 2, :].rearrange("p (a b) -> p a b", a=2), xs,
                                ALU.add).then_inc(bank_free, 1)
                freed(u)

            def squares(parts):
                for src in parts:
                    q = pos.n("sq")
                    wait(dve, sq_used, q - 1)
                    V.tensor_tensor(sq_buf[0:src.shape[0], q % 2, 0:src.shape[1]], src, src,
                                    ALU.mult).then_inc(sq_ready, 1)
                    pos.n("sq", 1)

            def small_unit():
                u = pos.n("su", 1)
                dve.wait_ge(small_done, u)
                return 2 + (u - 1) % 6

            def free_small(ins):
                ins.then_inc(small_free, 1)
                dve.wait_ge(small_free, pos.n("su"))

            def root(rows, n, factor, eps=EPS):
                b = small_unit()
                free_small(V.tensor_scalar(row_t[0:rows, 0:n], psum[0:rows, b, 0:n], factor, eps, ALU.mult, ALU.add))
                ask(V.reciprocal(row_t[0:rows, 0:n], row_t[0:rows, 0:n]))

            def split(c, cols, t, shift=None):
                if shift is None:
                    k = do(V.tensor_copy(hh[:, c, cols], t))
                    after(k)
                    V.tensor_tensor(hl[:, c, cols], t, hh[:, c, cols].bitcast(F32), ALU.subtract).then_inc(h_ready, 1)
                else:
                    k = do(V.tensor_scalar(hh[:, c, cols], t, shift, None, ALU.add))
                    after(k)
                    V.scalar_tensor_tensor(hl[:, c, cols], t, shift, hh[:, c, cols].bitcast(F32), ALU.add,
                                           ALU.subtract).then_inc(h_ready, 1)
                pos.n("h", 1)

            def norm(parts, factor, halves):
                n = parts[0].shape[1]
                squares(parts)
                root(P, n, factor)
                for cols, gain, shift, c0 in halves:
                    for c in range(0, len(parts), 2):
                        some = range(c, min(c + 2, len(parts)))
                        tmps = [tmp_buf[:, (pos.n("tmp", 1) - 1) % 4, :] for k in some]
                        ks = [do(V.scalar_tensor_tensor(t, parts[k][:, cols], gain(k), row_t[:, cols],
                                                        ALU.mult, ALU.mult)) for k, t in zip(some, tmps)]
                        for k, kk, t in zip(some, ks, tmps):
                            after(kk)
                            split(c0 + k, cols, t, shift(k) if shift else None)
                dve.wait_ge(h_ready, pos.n("h"))

            def plain_norm(name, i):
                norm([x[:, c, 0:T] for c in range(DC)], 1.0,
                     [(slice(0, T), lambda c: vec(name, DC * i + c), None, 0)])

            def head_norms(parts, rows, n, gains):
                squares([v for v in parts])
                root(rows, n, 1.0)
                tell_pe(V.tensor_copy(row_t[0:rows, 0:n], row_t[0:rows, 0:n]))
                for v, g in zip(parts, gains):
                    b = small_unit()
                    m, w = v.shape
                    free_small(V.scalar_tensor_tensor(v, v, g, psum[0:m, b, 0:w], ALU.mult, ALU.mult))

            def softmax_jobs(jobs):
                base = pos.n("jobs")
                for k in range(len(jobs) + 4):
                    if k < len(jobs):
                        j, job = base + k, jobs[k]
                        L, bf = job["L"], j % 2
                        sb_, mx, nm = s_buf[:, bf, 0:L], small[:, bf:bf + 1], small[:, 4 + bf:5 + bf]
                        ps = psum[:, 2 + bf, 0:L]
                        wait(dve, exp_done, j - 1)
                        if job["fox"]:
                            h, t = job["fox"]
                            kk = do(V.scalar_tensor_tensor(sb_, f_mask[:, t, :], ci[:, t, h:h + 1], cj[:, h, :],
                                                           ALU.add, ALU.subtract))
                            dve.wait_ge(score_done, j + 1)
                            after(kk)
                            step(V.scalar_tensor_tensor(sb_, ps, job["scale"], sb_, ALU.mult, ALU.add))
                            src, sc = sb_, 1.0
                        elif job["bias"] is not None:
                            dve.wait_ge(score_done, j + 1)
                            do(V.scalar_tensor_tensor(sb_[:, 0:T], ps[:, 0:T], job["scale"], job["bias"],
                                                      ALU.mult, ALU.add))
                            step(V.tensor_scalar(sb_[:, T:L], ps[:, T:L], job["scale"], None, ALU.mult))
                            src, sc = sb_, 1.0
                        else:
                            dve.wait_ge(score_done, j + 1)
                            src, sc = ps, job["scale"]
                        step(V.reduce_max(mx, src, AX_X))
                        if job["sink"] is not None:
                            step(V.tensor_scalar(mx, mx, sc, job["sink"], ALU.mult, ALU.max))
                            sc = 1.0
                        V.tensor_scalar(nm, mx, -sc, None, ALU.mult).then_inc(score_in, 1)
                    if 1 <= k <= len(jobs):
                        j, job = base + k - 1, jobs[k - 1]
                        L, bf = job["L"], j % 2
                        tot, rec = small[:, 8 + bf:9 + bf], small[:, 12 + bf:13 + bf]
                        dve.wait_ge(exp_done, j + 1)
                        if job["sink"] is not None:
                            step(V.tensor_tensor(tot, tot, small[:, 20 + bf:21 + bf], ALU.add))
                        step(V.reciprocal(rec, tot))
                        V.tensor_scalar(p_buf[:, j % 3, 0:L], p_buf[:, j % 3, 0:L], rec, None,
                                        ALU.mult).then_inc(prob_ready, 1)
                    if k >= 4 and (k - 4) % 4 == 3:
                        j, job = base + k - 4, jobs[k - 4]
                        o = psum[:, 6 + (j // 4) % 2, 0:T]
                        dve.wait_ge(pv_done, j + 1)
                        c, col = job["y"]
                        step(V.tensor_copy(hh[:, c, col:col + T], o))
                        V.tensor_tensor(hl[:, c, col:col + T], o, hh[:, c, col:col + T].bitcast(F32),
                                        ALU.subtract).then_inc(y_ready, 1)
                        pos.n("y", 1)
                dve.wait_ge(y_ready, pos.n("y"))
                pos.n("jobs", len(jobs))

            def evac_copies(copies, e):
                dve.wait_ge(gemm_done, e)
                for n, (dst, src) in enumerate(copies):
                    ins = V.tensor_copy(dst, src)
                    if n == len(copies) - 1:
                        ins.then_inc(bank_free, 1)
                freed(pos.u)
                pos.u += 1
                pos.e += 1

            def proj(units, last=False):
                lo_next(0, 0, 1)
                pos.p += 1
                for unit in units:
                    evac_copies(unit(pos.u % 2), pos.e + 1)

            V.memset(small[:, 60:61], 0.0).then_inc(bank_free, 1)
            V.memset(small[:, 61:62], 0.0).then_inc(bank_free, 1)
            lo(0, 0, SLOT)
            dve.wait_ge(base_loaded, 48)
            cond = vecs[:, VOFF["cond"]:VOFF["cond"] + 16]
            ask(V.memset(small[:, 62:63], 0.0))
            step(V.scalar_tensor_tensor(small[:, 24:40], small[:, 24:40], 1.0, cond, ALU.add, ALU.mult))
            tell_pe(V.tensor_scalar(cond_s[:].rearrange("p a b -> p (a b)"), small[:, 24:40], 0.5, None, ALU.mult))

            def ffn(f, peel=0):
                stage(11, 2, 1, 2, swiglu_evac(), peel=peel)
                pos.n("fseq", 44)
                pos.n("tanh", 22)
                pos.n("g", 22)
                residual = residual_evac(0.25, 2)

                def evac(i, j):
                    residual(i, j)
                    if f == 3 and j == 3:
                        ada_evac(44 + i)
                stage(4, 4, 1, 2, evac, w=FH * P)

            def hybrid():
                halves = lambda b: psum[:, b, :].rearrange("p (a b) -> p a b", a=2)
                for k in range(2):
                    proj([lambda b, k=k: [(u_pad[:, 2 * k:2 * k + 2, 3:3 + T], halves(b))]])
                for k in range(2):
                    proj([lambda b, k=k: [(gate_t[:, 2 * k:2 * k + 2, :], halves(b))]])
                for k in range(4):
                    proj([lambda b, k=k: [(f_qk[:, 2 * k:2 * k + 2, :], halves(b))]])
                for k in range(2):
                    proj([lambda b, k=k: [(f_v[:, :, k * T:(k + 1) * T], halves(b))]])
                dve.wait_ge(phase_loaded[0], 16)
                lam = vecs[:, VOFF["lam"]:VOFF["lam"] + 4]
                u_, w_, q_, sp4 = small[:, 44:48], small[:, 48:52], small[:, 52:56], small[:, 56:60]
                step(V.tensor_scalar(q_, lam, -1.0, None, ALU.mult))
                ask(V.tensor_tensor(u_, q_, lam, ALU.min))
                step(V.tensor_scalar(w_, u_, 1.0, None, ALU.add))
                step(V.tensor_scalar(sp4, w_, -1.0, 1e-30, ALU.add, ALU.max))
                step(V.reciprocal(sp4, sp4))
                step(V.tensor_tensor(u_, u_, sp4, ALU.mult))
                ask(V.tensor_scalar(q_, q_, 0.0, None, ALU.max))
                step(V.tensor_tensor(w_, w_, u_, ALU.mult))
                step(V.tensor_tensor(w_, w_, q_, ALU.add))
                step(V.tensor_scalar(sp4, w_, -4.0, None, ALU.mult))
                gb = small[:, 24:32]
                step(V.tensor_scalar(gb, vecs[:, VOFF["gate_b"]:VOFF["gate_b"] + 8], 0.5, None, ALU.mult))
                step(V.memset(u_pad[:, :, 0:3], 0.0))
                cw = lambda j, c: vec("conv_w", 4 * j + c)
                for c in range(4):
                    last = do(V.tensor_scalar(xc[:, c, :], u_pad[:, c, 3:3 + T], cw(3, c), vec("conv_b", c),
                                              ALU.mult, ALU.add))
                for j in range(3):
                    for c in range(4):
                        after(pos.n("seq") - 3)
                        last = do(V.scalar_tensor_tensor(xc[:, c, :], u_pad[:, c, j:j + T], cw(j, c), xc[:, c, :],
                                                         ALU.mult, ALU.add))
                after(last)
                tell_pe(V.memset(small[:, 63:64], 0.0))
                for c in range(4):
                    b = small_unit()
                    free_small(V.tensor_scalar(ra[:, c, :], psum[:, b, 0:T], vec("gate_b", c), None, ALU.add))
                    b = small_unit()
                    free_small(V.tensor_scalar(ia[:, c, :], psum[:, b, 0:T], vec("gate_b", 4 + c), None, ALU.add))
                    ask(V.memset(small[:, 63:64], 0.0))
                    ask(V.memset(small[:, 63:64], 0.0))
                for c in range(4):
                    last = do(V.tensor_scalar(ra[:, c, :], ra[:, c, :], 1.0, sp4[:, c:c + 1], ALU.add, ALU.mult))
                after(last)
                ask(V.memset(small[:, 63:64], 0.0))
                ask(V.memset(small[:, 63:64], 0.0))
                a2 = lf_big
                step(V.tensor_tensor(a2, ra[:, :, :], ra[:, :, :], ALU.mult))
                step(V.scalar_tensor_tensor(th[:, :, :], a2, 1.0, th[:, :, :], ALU.add, ALU.mult))
                ask(V.tensor_scalar(th[:, :, :], th[:, :, :], -1.0, 1e-34, ALU.mult, ALU.max))
                step(V.scalar_tensor_tensor(ia[:, :, :], ia[:, :, :], 1.0, xc[:, :, :], ALU.add, ALU.mult))
                step(V.scalar_tensor_tensor(ia[:, :, :], ia[:, :, :], 0.5, th[:, :, :], ALU.mult, ALU.mult))
                for c in range(4):
                    last = do(V.tensor_tensor_scan(th[:, c, :], ra[:, c, :], ia[:, c, :], 0.0, ALU.mult, ALU.add))
                step(V.tensor_tensor(xc[:, :, :], gate_t[:, :, :], gate_t[:, :, :], ALU.mult))
                step(V.tensor_scalar(xc[:, :, :], xc[:, :, :], 0.044715, 1.0, ALU.mult, ALU.add))
                ask(V.tensor_tensor(xc[:, :, :], xc[:, :, :], gate_t[:, :, :], ALU.mult))
                step(V.scalar_tensor_tensor(ra[:, :, :], ra[:, :, :], 1.0, gate_t[:, :, :], ALU.add, ALU.mult))
                step(V.scalar_tensor_tensor(ra[:, :, :], ra[:, :, :], 0.5, th[:, :, :], ALU.mult, ALU.mult))
                b = small_unit()
                free_small(V.tensor_scalar(lf[0:8, 0, :], psum[0:8, b, 0:T], vec("fox_fb", 0, 8), None, ALU.add))
                step(V.tensor_scalar(lf[0:8, 1, :], lf[0:8, 0, :], -1.0, None, ALU.mult))
                ask(V.tensor_tensor(lf[0:8, 1, :], lf[0:8, 1, :], lf[0:8, 0, :], ALU.min))
                ask(V.memset(ones_r[0:8, :], 1.0))
                step(V.scalar_tensor_tensor(lf[0:8, 0, :], lf[0:8, 0, :], 0.0, lf[0:8, 1, :], ALU.min, ALU.subtract))
                tell_pe(V.tensor_tensor_scan(lf[0:8, 1, :], ones_r[0:8, :], lf[0:8, 0, :], 0.0, ALU.mult, ALU.add))
                b = small_unit()
                free_small(V.tensor_copy(ci[:, :, :], psum[:, b, 0:16].rearrange("p (a b) -> p a b", a=2)))
                for h in range(4):
                    b = small_unit()
                    free_small(V.tensor_copy(cj[:, 2 * h:2 * h + 2, :],
                                             psum[:, b, :].rearrange("p (a b) -> p a b", a=2)))
                head_norms([f_qk[:, c, :] for c in range(8)], 16, T, [vec("fox_g", int(c >= 4)) for c in range(8)])
                for c in range(4):
                    split(c, slice(0, T), ra[:, c, :])
                dve.wait_ge(h_ready, pos.n("h"))
                tell_pe(V.memset(small[:, 63:64], 0.0))
                softmax_jobs(list(fox_jobs()))
                stage(2, 2, 1, 2, pair_evac)

            def stick():
                base_q = s_qk

                def evac_qk(i, j):
                    u = pos.u + 2 * i + j
                    dve.wait_ge(gemm_done, pos.e + 2 * i + j + 1)
                    k = 2 * i + j
                    V.tensor_copy(base_q[:, bass.ds(2 * k, 2), :] if not isinstance(k, int) else base_q[:, 2 * k:2 * k + 2, :],
                                  psum[:, (pos.u + j) % 2, :].rearrange("p (a b) -> p a b", a=2)).then_inc(bank_free, 1)
                stage(4, 2, 1, 2, evac_qk)

                def evac_v(i, j):
                    dve.wait_ge(gemm_done, pos.e + 2 * i + j + 1)
                    k = 2 * i + j
                    V.tensor_copy(s_v[:, :, bass.ds(k * T, T)] if not isinstance(k, int) else s_v[:, :, k * T:(k + 1) * T],
                                  psum[:, (pos.u + j) % 2, :].rearrange("p (a b) -> p a b", a=2)).then_inc(bank_free, 1)
                stage(2, 2, 1, 2, evac_v)
                dve.wait_ge(phase_loaded[1], 16)
                for h in range(16 + 4):
                    if h < 16:
                        dve.wait_ge(sb_z_done, h + 1)
                        wait(dve, sb_w_done, h - 3)
                        z = sb_z[:, h % 4, :]
                        step(V.scalar_tensor_tensor(z, psum[:, 2 + h % 2, 0:384], HD ** -0.5, s_mask[:],
                                                    ALU.mult, ALU.add))
                        V.scalar_tensor_tensor(sb_e[:, h % 2, :], z, -1.0, z, ALU.mult, ALU.max).then_inc(sb_z_in, 1)
                    if 1 <= h <= 16:
                        g = h - 1
                        dve.wait_ge(sb_e_done, 2 * g + 2)
                        wait(dve, sb_i_done, g - 1)
                        V.scalar_tensor_tensor(sb_n[:, g % 2, :], sb_z[:, g % 4, :], 0.0, sb_e[:, g % 2, :], ALU.max,
                                               ALU.add).then_inc(sb_n_in, 1)
                    if 2 <= h <= 17:
                        g = h - 2
                        dve.wait_ge(sb_i_done, g + 1)
                        V.tensor_tensor(sb_z[:, g % 4, :], psum[:, 4 + g % 2, 0:384], sb_z[:, g % 4, :],
                                        ALU.add).then_inc(sb_i_in, 1)
                    if h >= 4 and h % 2 == 1:
                        g = h - 4
                        o = psum[:, 6 + (g // 2) % 2, 0:T]
                        dve.wait_ge(sb_o_done, g + 1)
                        step(V.tensor_copy(hh[:, g // 2, 0:T], o))
                        V.tensor_tensor(hl[:, g // 2, 0:T], o, hh[:, g // 2, 0:T].bitcast(F32),
                                        ALU.subtract).then_inc(sb_y, 1)
                dve.wait_ge(sb_y, 8)
                stage(2, 2, 1, 2, pair_evac)

            def mod(layer, what, c, who):
                return mods[:, 48 * layer + 8 * what + c, who:who + 1]

            def derive(layer, which, name, who, slot):
                c0 = 48 * layer + 8 * (1 + 3 * which)
                g = vecs[:, VOFF[name] + 8 * layer:VOFF[name] + 8 * layer + 8]
                step(V.scalar_tensor_tensor(gmod[:, slot, :], mods[:, c0:c0 + 8, who], 1.0, g, ALU.add, ALU.mult))

            def mod_norm(layer, which, whos):
                name = ("norm_mix", "norm_mlp")[which]
                for who in whos:
                    derive(layer, which, name, who, who)
                norm([x[:, c, 0:T * len(whos)] for c in range(DC)], 1.0,
                     [(slice(T * who, T * who + T), lambda c, who=who: gmod[:, who, c:c + 1],
                       lambda c, who=who: mod(layer, 3 * which, c, who), 0) for who in whos])

            def gated_unit(c, bank, e, u, layer, what, joint):
                dve.wait_ge(gemm_done, e)
                m = 48 * layer + 8 * what + c
                for who in range(2 if joint else 1):
                    cols = slice(T * who, T * who + T)
                    g = mods[:, m, who:who + 1] if isinstance(c, int) else \
                        mods[:, bass.ds(m, 1), who:who + 1].rearrange("p a b -> p (a b)")
                    xs = pick(x, c, cols)
                    ins = V.scalar_tensor_tensor(xs, psum[:, bank, cols], g, xs, ALU.mult, ALU.add)
                ins.then_inc(bank_free, 1)
                freed(u)

            def even():
                for k in range(2):
                    proj([lambda b, k=k, m=m: [(e_qk[:, 2 * k + m, :], psum[:, b, :])] for m in range(2)])
                proj([lambda b: [(e_qk[:, 4, :], psum[:, b, :])],
                      lambda b: [(a_v[:, :, :], psum[:, b, :].rearrange("p (a b) -> p a b", a=4))]])
                for k in range(4):
                    proj([lambda b, k=k, m=m: [(e_qk[:, 5 + 2 * k + m, :], psum[:, b, :])] for m in range(2)])
                for k in range(2):
                    proj([lambda b, k=k, m=m: [(b_v[:, 2 * m:2 * m + 2, k * T:(k + 1) * T],
                                                psum[:, b, :].rearrange("p (a b) -> p a b", a=2))] for m in range(2)])
                dve.wait_ge(phase_loaded[2], 32)
                gains = [vec("a_qn")] * 4 + [vec("a_kn")] + [vec("b_qn")] * 4 + [vec("b_kn")] * 4
                head_norms([e_qk[:, c, :] for c in range(13)], 26, TJ, gains)
                tell_pe(V.memset(small[:, 63:64], 0.0))
                for c in range(5):
                    b = small_unit()
                    free_small(V.tensor_tensor(tmp_buf[:, c % 4, :], psum[:, b, 0:T], sin_a[:], ALU.mult))
                    step(V.tensor_tensor(e_qk[:, c, 0:T], e_qk[:, c, 0:T], cos_a[:], ALU.mult))
                    step(V.tensor_tensor(e_qk[:, c, 0:T], e_qk[:, c, 0:T], tmp_buf[:, c % 4, :], ALU.add))
                for g in range(2):
                    for half in range(2):
                        step(V.tensor_copy(k_dup[64 * half:64 * half + 64, g, :], e_qk[64 * g:64 * g + 64, 4, :]))
                dve.wait_ge(bias_loaded, 16)
                for h in range(8):
                    for t in range(2):
                        step(V.tensor_tensor(b_bias[:, t, h, :], b_bias[:, t, h, :], col_mask[:], ALU.add))
                tell_pe(V.memset(small[:, 63:64], 0.0))
                softmax_jobs(list(even_jobs()))

                def evac(i, j):
                    for m in range(2):
                        u = pos.u + 4 * i + 2 * j + m
                        gated_unit(4 * i + 2 * j + m, (pos.u + m) % 2, pos.e + 4 * i + 2 * j + m + 1, u, 0, 2, True)
                stage(2, 2, 2, 4, evac)

            def relu2(bank, e, u, dst, fs, gn):
                dve.wait_ge(gemm_done, e)
                V.tensor_scalar(mlp_r[:], psum[:, bank, :], 0.0, None, ALU.max).then_inc(bank_free, 1)
                freed(u)
                V.tensor_tensor(mlp_g[:], mlp_r[:], mlp_r[:], ALU.mult).then_inc(ffn_seq, 1)
                dve.wait_ge(ffn_seq, fs + 1)
                V.tensor_copy(flat(gh, dst, 512), mlp_g[:]).then_inc(ffn_seq, 1)
                dve.wait_ge(ffn_seq, fs + 2)
                V.tensor_tensor(flat(gl, dst, 512), mlp_g[:], flat(gh, dst, 512).bitcast(F32),
                                ALU.subtract).then_inc(g_ready, 1)
                dve.wait_ge(g_ready, gn)

            def mlp_joint():
                fb, gb = pos.n("fseq"), pos.n("g")

                def evac(i, j):
                    for m in range(2):
                        k = 4 * i + 2 * j + m
                        relu2((pos.u + m) % 2, pos.e + k + 1, pos.u + k, k * 512, fb + 2 * k, gb + k + 1)
                stage(4, 2, 2, 4, evac)
                pos.n("fseq", 32)
                pos.n("g", 16)

                def evac_out(i, j):
                    k = 2 * i + j
                    gated_unit(k, (pos.u + j) % 2, pos.e + k + 1, pos.u + k, 0, 5, True)
                stage(4, 2, 1, 2, evac_out)

            def mlp_latent():
                fb, gb = pos.n("fseq"), pos.n("g")

                def evac(i, j):
                    k = 2 * i + j
                    relu2((pos.u + j) % 2, pos.e + k + 1, pos.u + k, k * 512, fb + 2 * k, gb + k + 1)
                stage(8, 2, 1, 2, evac)
                pos.n("fseq", 32)
                pos.n("g", 16)

                def evac_out(i, j):
                    if j % 2:
                        k = 2 * i + j // 2
                        gated_unit(k, (pos.u + j // 2) % 2, pos.e + 4 * i + j + 1, pos.u + k, 1, 5, False)
                stage(4, 4, 1, 2, evac_out, last=True)

            def latent():
                proj([lambda b, m=m: [(lat_c[:, m, :], psum[:, b, 0:T])] for m in range(2)])
                proj([lambda b: [(lat_c[:, 2, :], psum[:, b, 0:T])], lambda b: [(lat_kv[:, 0, :], psum[:, b, :])]])
                proj([lambda b: [(lat_kv[:, 1, :], psum[:, b, :])],
                      lambda b: [(m_k[64:96, 0, :], psum[96:128, b, :])]])
                norm([lat_c[:, c, :] for c in range(3)], D / 384,
                     [(slice(0, T), lambda c: vec("qa_norm", c), None, 0)])
                norm([lat_kv[:, c, :] for c in range(2)], D / 256,
                     [(slice(T * w, T * w + T), lambda c: vec("kva_norm", c), None, 3) for w in range(2)])
                h = 0
                for n in (3, 3, 2):
                    proj([lambda b, h=h, m=m: [(m_q[0:MQ, h + 2 * m:h + 2 * m + 2, :],
                                                psum[0:MQ, b, :].rearrange("p (a b) -> p a b", a=2))]
                          for m in range(n)])
                    h += 2 * n
                for k in range(2):
                    proj([lambda b, k=k, m=m: [(m_k[0:64, 8 * k + m, :], psum[0:64, b, :])] for m in range(8)] +
                         [lambda b, k=k, m=m: [(m_v[:, m, 512 * k:512 * k + 512], psum[:, b, :])] for m in range(4)])
                dve.wait_ge(phase_loaded[3], 16)
                head_norms([m_q[0:MQ, h, :] for h in range(16)], 32, T, [vec("qn", 0, MQ)] * 16)
                head_norms([m_k[0:MQ, 0, :]] + [m_k[0:HD, h, :] for h in range(1, 16)], 32, TJ,
                           [vec("kn", 0, MQ)] + [vec("kn", 0, HD)] * 15)
                tell_pe(V.memset(small[:, 63:64], 0.0))
                for part in range(9):
                    v = (m_q[64:96, 2 * part:2 * part + 2, :] if part < 8 else m_k[64:96, 0:1, 0:T])
                    n = v.shape[1]
                    b = small_unit()
                    sn = sin_m[64:96, :].unsqueeze(1).broadcast_to([MR, n, T])
                    cn = cos_m[64:96, :].unsqueeze(1).broadcast_to([MR, n, T])
                    t_ = sq_buf[64:96, 0, 0:n * T].rearrange("p (a b) -> p a b", a=n)
                    free_small(V.tensor_tensor(t_, psum[64:96, b, 0:n * T].rearrange("p (a b) -> p a b", a=n), sn,
                                               ALU.mult))
                    step(V.tensor_tensor(v, v, cn, ALU.mult))
                    step(V.tensor_tensor(v, v, t_, ALU.add))
                V.memset(small[:, 63:64], 0.0).then_inc(to_act, 1)
                pos.n("ask_only", 1)
                dve.wait_ge(krope_done, 15)
                tell_pe(V.memset(small[:, 62:63], 0.0))
                softmax_jobs(list(latent_jobs()))

                def evac(i, j):
                    u = pos.u + 2 * i + j
                    dve.wait_ge(gemm_done, pos.e + 2 * i + j + 1)
                    k = 2 * i + j
                    for m in range(2):
                        c = 2 * k + m
                        col = 48 + 16 + c
                        g = mods[:, col, 0:1] if isinstance(c, int) else \
                            mods[:, bass.ds(col, 1), 0:1].rearrange("p a b -> p (a b)")
                        xs = pick(x, c, slice(0, T))
                        ins = V.scalar_tensor_tensor(xs, psum[:, (pos.u + j) % 2, T * m:T * m + T], g, xs,
                                                     ALU.mult, ALU.add)
                    ins.then_inc(bank_free, 1)
                    freed(u)
                stage(2, 2, 1, 2, evac)

            lf_big = scr[:, 0:1024].rearrange("p (a b) -> p a b", a=4)
            plain_norm("ffn_norm", 0)
            ffn(0, peel=1)
            plain_norm("mix_norm", 0)
            hybrid()
            plain_norm("ffn_norm", 1)
            ffn(1)
            plain_norm("ffn_norm", 2)
            ffn(2)
            plain_norm("mix_norm", 1)
            stick()
            plain_norm("ffn_norm", 3)
            ffn(3)

            dve.wait_ge(bank_free, pos.u + 2)
            dve.wait_ge(ada_in, ADA_PANELS)
            mod_norm(0, 0, (0, 1))
            even()
            mod_norm(0, 1, (0, 1))
            mlp_joint()
            mlp_joint()
            mod_norm(1, 0, (0, 1))
            latent()
            mod_norm(1, 1, (0,))
            mlp_latent()

        @block.tensor
        def _(pe):
            pos = Pos()
            mm = nc.tensor.matmul

            def told(n=1):
                pe.wait_ge(to_pe, pos.n("to_pe", n))

            def product(out, pairs):
                for n, (sh, sl, mh, ml) in enumerate(pairs):
                    mm(out, sh, mh, start=n == 0, stop=False)
                    mm(out, sh, ml, start=False, stop=False)
                    ins = mm(out, sl, mh, start=False, stop=n == len(pairs) - 1)
                return ins

            def panel(rel, i, per_iter):
                base = pos.p + rel
                pe.wait_ge(lo_ready, 2 * (base + per_iter * i + 1))
                return base % 2

            def bank(u):
                pe.wait_ge(bank_free, u + 1)

            def stage(n, per_iter, ev, units, work, peel=0):
                def body(i):
                    for j in range(per_iter):
                        work(i, j, panel(j, i, per_iter))
                loop(pe, n, body, peel)
                pos.p += n * per_iter
                pos.e += ev * n * per_iter
                pos.u += units * n

            def wtile(s, k, c, width):
                a = k * width + c * P
                return wh[s][:, a:a + P], wl[s][:, a:a + P]

            def two_chunks(out, s, n=T, done=True):
                for m in range(2):
                    ins = product(out[:, m * n:(m + 1) * n],
                                  [(*wtile(s, k, m, 2 * P), hh[:, k, 0:n], hl[:, k, 0:n]) for k in range(DC)])
                return ins

            def ffn(f, peel=0):
                ab = pos.n("ada", 11) - 11

                def into(i, j, s):
                    bank(pos.u + 2 * i + j)
                    two_chunks(psum[:, (pos.u + j) % 2, :], s).then_inc(gemm_done, 1)
                    if j == 1:
                        ada(ab + i)
                pe.wait_ge(h_ready, pos.n("h"))
                stage(11, 2, 1, 2, into, peel=peel)
                pe.wait_ge(g_ready, pos.n("g", 22))

                def out_of(i, j, s):
                    half = j % 2
                    if half == 0:
                        bank(pos.u + 2 * i + j // 2)
                    out = psum[:, (pos.u + j // 2) % 2, 0:T]
                    for k in range(FH):
                        a, g0 = k * P, (half * FH + k) * T
                        first, last = half == 0 and k == 0, half == 1 and k == FH - 1
                        mm(out, wh[s][:, a:a + P], gh[:, g0:g0 + T], start=first, stop=False)
                        mm(out, wh[s][:, a:a + P], gl[:, g0:g0 + T], start=False, stop=False)
                        ins = mm(out, wl[s][:, a:a + P], gh[:, g0:g0 + T], start=False, stop=last)
                    ins.then_inc(gemm_done, 1)
                    if f == 3 and j == 3:
                        ada(44 + i)
                stage(4, 4, 1, 2, out_of)
                pe.wait_ge(ada_in, ab + 11 + (4 if f == 3 else 0))

            def ada(k):
                pe.wait_ge(ada_loaded, 16 * k + 16)
                wait(pe, ada_in, k)
                for m in range(2):
                    for c in range(DC):
                        a = c * 2 * P + m * P
                        ins = mm(psum[:, ADA_BANK, 2 * m:2 * m + 2], raw_a[:, a:a + P], cond_s[:, c, :],
                                 start=c == 0, stop=c == DC - 1)
                ins.then_inc(ada_done, 1)

            def sums(tables, n, rows, last_rows=None):
                u = pos.n("su", 1)
                wait(pe, small_free, u - 6)
                out = psum[0:rows, 2 + (u - 1) % 6, 0:n]
                for k, t in enumerate(tables):
                    q = pos.n("sq", 1)
                    pe.wait_ge(sq_ready, q)
                    ins = mm(out, t, sq_buf[0:t.shape[0], (q - 1) % 2, 0:n], start=k == 0, stop=k == len(tables) - 1)
                    ins.then_inc(sq_used, 1)
                pe.wait_ge(sq_used, pos.n("sq"))
                pe.sem_inc(small_done, 1)

            def small_out():
                u = pos.n("su", 1)
                wait(pe, small_free, u - 6)
                return 2 + (u - 1) % 6

            def norm(n, chunks=DC, halves=1):
                sums([mean_w] * chunks, n, P)
                pos.n("h", chunks * halves)

            def head_norms(parts, rows, n, sel, bsel):
                sums([sel(c) for c in range(len(parts))], n, rows)
                told()
                for c, (m, w) in enumerate(parts):
                    b = small_out()
                    mm(psum[0:m, b, 0:w], bsel(c, m), row_t[0:rows, 0:w], start=True, stop=True).then_inc(small_done, 1)

            def softmax_jobs(jobs):
                base = pos.n("jobs")
                for k in range(len(jobs) + 3):
                    if k < len(jobs):
                        j, job = base + k, jobs[k]
                        wait(pe, exp_done, j - 1)
                        mm(psum[:, 2 + j % 2, 0:job["L"]], job["q"], job["k"], start=True,
                           stop=True).then_inc(score_done, 1)
                    if 2 <= k <= len(jobs) + 1:
                        j, job = base + k - 2, jobs[k - 2]
                        pe.wait_ge(prob_ready, j + 1)
                        wait(pe, turn_in, j - 1)
                        for b in range(job["L"] // P):
                            ins = nc.tensor.transpose(psum[:, 4 + j % 2, b * P:(b + 1) * P],
                                                      p_buf[:, j % 3, b * P:(b + 1) * P], ident)
                        ins.then_inc(turn_done, 1)
                    if k >= 3:
                        j, job = base + k - 3, jobs[k - 3]
                        pe.wait_ge(turn_in, j + 1)
                        if j % 4 == 0:
                            wait(pe, y_ready, j // 4 - 1)
                        r0 = 64 * (job["h"] % 2)
                        out = psum[r0:r0 + 64, 6 + (j // 4) % 2, job["t"] * P:(job["t"] + 1) * P]
                        for b, v in enumerate(job["v"]):
                            ins = mm(out, v, pt_buf[:, j % 2, b * P:(b + 1) * P], start=b == 0,
                                     stop=b == len(job["v"]) - 1)
                        ins.then_inc(pv_done, 1)
                pos.n("jobs", len(jobs))
                pe.wait_ge(y_ready, pos.n("jobs") // 4)

            def unit():
                bank(pos.u)
                b = pos.u % 2
                pos.u += 1
                pos.e += 1
                return psum[:, b, :]

            def take():
                s = panel(0, 0, 1)
                pos.p += 1
                return s

            def chunk_unit(s, m, width, n, kc=DC, src=(hh, hl), k0=0, col=None):
                a0 = m * P if col is None else col
                out = unit()
                product(out[:, 0:n], [(wh[s][:, k * width + a0:k * width + a0 + P],
                                       wl[s][:, k * width + a0:k * width + a0 + P],
                                       hh[:, k0 + k, 0:n], hl[:, k0 + k, 0:n]) for k in range(kc)]).then_inc(gemm_done, 1)

            def token_tiles(s, tiles, col, cols, width):
                out = unit()
                for n, t in enumerate(tiles):
                    ins = product(out[:, n * cols:(n + 1) * cols],
                                  [(hh[:, k, t * P:(t + 1) * P], hl[:, k, t * P:(t + 1) * P],
                                    wh[s][:, k * width + col:k * width + col + cols],
                                    wl[s][:, k * width + col:k * width + col + cols]) for k in range(DC)])
                ins.then_inc(gemm_done, 1)

            def hybrid():
                pe.wait_ge(h_ready, pos.n("h"))
                for k in range(8):
                    s = take()
                    two_chunks(unit(), s).then_inc(gemm_done, 1)
                for k in range(2):
                    token_tiles(take(), (0, 1), 0, 2 * P, 2 * P)
                told()
                for c in range(4):
                    for g in range(2):
                        b = small_out()
                        mm(psum[:, b, 0:T], gw[:, g, c, :], xc[:, c, :], start=True, stop=True).then_inc(small_done, 1)
                b = small_out()
                for k in range(DC):
                    for n, part in enumerate((hh, hl)):
                        ins = mm(psum[0:8, b, 0:T], wf[:, k, :], part[:, k, 0:T].bitcast(F32),
                                 start=k == 0 and n == 0, stop=k == DC - 1 and n == 1)
                ins.then_inc(small_done, 1)
                told()
                b = small_out()
                for t in range(2):
                    ins = nc.tensor.transpose(psum[:, b, 8 * t:8 * t + 8], lf[0:8, 1, t * P:(t + 1) * P], ident[0:8, 0:8])
                ins.then_inc(small_done, 1)
                for h in range(4):
                    b = small_out()
                    for m in range(2):
                        ins = mm(psum[:, b, m * T:(m + 1) * T], f_eh[0:8, 2 * h + m, :], lf[0:8, 1, :], start=True,
                                 stop=True)
                    ins.then_inc(small_done, 1)
                head_norms([(P, T)] * 8, 16, T, lambda c: f_sel[:, c, :], lambda c, m: f_bsel[0:16, c, :])
                told()
                pos.n("h", 4)
                softmax_jobs(list(fox_jobs()))
                pe.wait_ge(h_ready, pos.n("h"))
                out_proj()

            def out_proj():
                def work(i, j, s):
                    bank(pos.u + 2 * i + j)
                    two_chunks(psum[:, (pos.u + j) % 2, :], s).then_inc(gemm_done, 1)
                stage(2, 2, 1, 2, work)

            def stick():
                pe.wait_ge(h_ready, pos.n("h"))

                def qk(i, j, s):
                    bank(pos.u + 2 * i + j)
                    two_chunks(psum[:, (pos.u + j) % 2, :], s).then_inc(gemm_done, 1)
                stage(4, 2, 1, 2, qk)

                def vv(i, j, s):
                    bank(pos.u + 2 * i + j)
                    out = psum[:, (pos.u + j) % 2, :]
                    for t in range(2):
                        ins = product(out[:, t * T:(t + 1) * T],
                                      [(hh[:, k, t * P:(t + 1) * P], hl[:, k, t * P:(t + 1) * P],
                                        wh[s][:, k * T:(k + 1) * T], wl[s][:, k * T:(k + 1) * T]) for k in range(DC)])
                    ins.then_inc(gemm_done, 1)
                stage(2, 2, 1, 2, vv)
                pe.wait_ge(bank_free, pos.u + 2)
                pe.wait_ge(phase_loaded[1], 16)
                for h in range(16 + 3):
                    if h < 16:
                        r, c = slice(64 * (h % 2), 64 * (h % 2) + 64), h // 2
                        wait(pe, sb_z_in, h - 1)
                        out = psum[:, 2 + h % 2, :]
                        mm(out[:, 0:T], s_qk[r, 8 + c, 0:P], s_qk[r, c, :], start=True, stop=True)
                        mm(out[:, T:T + P], s_qk[r, 8 + c, P:T], s_qk[r, c, P:T], start=True,
                           stop=True).then_inc(sb_z_done, 1)
                    if 1 <= h <= 16:
                        g = h - 1
                        b = g % 2
                        pe.wait_ge(sb_n_in, g + 1)
                        wait(pe, sb_i_in, g - 1)
                        out = psum[:, 4 + b, :]
                        mm(out[:, 0:P], s_tri[:], sb_n[:, b, 0:P], start=True, stop=True)
                        mm(out[:, P:T], s_tri[:], sb_n[:, b, P:T], start=True, stop=False)
                        mm(out[:, P:T], s_ones[:], sb_n[:, b, T:T + P], start=False, stop=True)
                        mm(out[:, T:T + P], s_tri[:], sb_n[:, b, T:T + P], start=True, stop=True).then_inc(sb_i_done, 1)
                    if h >= 3:
                        g = h - 3
                        b = g % 2
                        pe.wait_ge(sb_w_done, g + 1)
                        if g % 2 == 0:
                            wait(pe, sb_y, g // 2 - 1)
                        r0 = 64 * (g % 2)
                        o = psum[r0:r0 + 64, 6 + (g // 2) % 2, :]
                        mm(o[:, 0:P], s_v[:, 0, g * HD:(g + 1) * HD], sb_w[:, b, 0:P], start=True, stop=True)
                        mm(o[:, P:T], s_v[:, 0, g * HD:(g + 1) * HD], sb_w[:, b, P:T], start=True, stop=False)
                        mm(o[:, P:T], s_v[:, 1, g * HD:(g + 1) * HD], sb_w[:, b, T:T + P], start=False,
                           stop=True).then_inc(sb_o_done, 1)
                pe.wait_ge(sb_y, 8)
                out_proj()

            def joint_chunks(i, j, s, per_iter):
                for m in range(2):
                    bank(pos.u + 2 * per_iter * i + 2 * j + m)
                    product(psum[:, (pos.u + m) % 2, :],
                            [(*wtile(s, k, m, 2 * P), hh[:, k, :], hl[:, k, :]) for k in range(DC)]
                            ).then_inc(gemm_done, 1)

            def even():
                pe.wait_ge(h_ready, pos.n("h"))
                for k in range(9):
                    s = take()
                    if k == 2:
                        chunk_unit(s, 0, 2 * P, TJ)
                        token_tiles(s, range(4), P, P, 2 * P)
                    elif k < 7:
                        for m in range(2):
                            chunk_unit(s, m, 2 * P, TJ)
                    else:
                        token_tiles(s, (0, 1), 0, 2 * P, 2 * P)
                        token_tiles(s, (2, 3), 0, 2 * P, 2 * P)
                pe.wait_ge(phase_loaded[2], 32)
                head_norms([(P, TJ)] * 13, 26, TJ, lambda c: e_sel[:, c, 0:26], lambda c, m: e_bsel[0:26, c, :])
                told()
                for c in range(5):
                    b = small_out()
                    mm(psum[:, b, 0:T], rot_a[:], e_qk[:, c, 0:T], start=True, stop=True).then_inc(small_done, 1)
                told()
                softmax_jobs(list(even_jobs()))
                stage(2, 2, 2, 4, lambda i, j, s: joint_chunks(i, j, s, 2))

            def mlp_joint():
                stage(4, 2, 2, 4, lambda i, j, s: joint_chunks(i, j, s, 2))
                pe.wait_ge(g_ready, pos.n("g", 16))

                def out_of(i, j, s):
                    bank(pos.u + 2 * i + j)
                    product(psum[:, (pos.u + j) % 2, :],
                            [(wh[s][:, k * P:(k + 1) * P], wl[s][:, k * P:(k + 1) * P],
                              gh[:, k * TJ:(k + 1) * TJ], gl[:, k * TJ:(k + 1) * TJ]) for k in range(16)]
                            ).then_inc(gemm_done, 1)
                stage(4, 2, 1, 2, out_of)

            def mlp_latent():
                pe.wait_ge(h_ready, pos.n("h"))

                def into(i, j, s):
                    bank(pos.u + 2 * i + j)
                    two_chunks(psum[:, (pos.u + j) % 2, :], s).then_inc(gemm_done, 1)
                stage(8, 2, 1, 2, into)
                pe.wait_ge(g_ready, pos.n("g", 16))

                def out_of(i, j, s):
                    half = j % 2
                    if half == 0:
                        bank(pos.u + 2 * i + j // 2)
                    out = psum[:, (pos.u + j // 2) % 2, 0:T]
                    for k in range(16):
                        a, g0 = k * P, (half * 16 + k) * T
                        first, last = half == 0 and k == 0, half == 1 and k == 15
                        mm(out, wh[s][:, a:a + P], gh[:, g0:g0 + T], start=first, stop=False)
                        mm(out, wh[s][:, a:a + P], gl[:, g0:g0 + T], start=False, stop=False)
                        ins = mm(out, wl[s][:, a:a + P], gh[:, g0:g0 + T], start=False, stop=last)
                    ins.then_inc(gemm_done, 1)
                stage(4, 4, 1, 2, out_of)

            def latent():
                pe.wait_ge(h_ready, pos.n("h"))
                s = take()
                chunk_unit(s, 0, 2 * P, T)
                chunk_unit(s, 1, 2 * P, T)
                s = take()
                chunk_unit(s, 0, 2 * P, T)
                chunk_unit(s, 1, 2 * P, TJ)
                s = take()
                chunk_unit(s, 0, 160, TJ)
                chunk_unit(s, 0, 160, TJ, col=32)
                norm(T, 3)
                norm(TJ, 2, 2)
                pe.wait_ge(h_ready, pos.n("h"))
                for n in (3, 3, 2):
                    s, width = take(), 2 * n * MQ
                    for m in range(n):
                        out = unit()
                        for r in range(2):
                            a = (2 * m + r) * MQ
                            ins = product(out[0:MQ, r * T:(r + 1) * T],
                                          [(wh[s][:, k * width + a:k * width + a + MQ],
                                            wl[s][:, k * width + a:k * width + a + MQ],
                                            hh[:, k, 0:T], hl[:, k, 0:T]) for k in range(3)])
                        ins.then_inc(gemm_done, 1)
                for k in range(2):
                    s = take()
                    for m in range(8):
                        chunk_unit(s, m, D, TJ, kc=2, k0=3)
                    wv = [w[s][:].rearrange("p (k h d) -> p k h d", k=2, d=P) for w in (wh, wl)]
                    for t in range(4):
                        out = unit()
                        product(out[:, :], [(hh[:, 3 + kk, t * P:(t + 1) * P], hl[:, 3 + kk, t * P:(t + 1) * P],
                                             wv[0][:, kk, :, HD:P], wv[1][:, kk, :, HD:P]) for kk in range(2)]
                                ).then_inc(gemm_done, 1)
                pe.wait_ge(phase_loaded[3], 16)
                head_norms([(MQ, T)] * 16, 32, T, lambda c: m_sel[0:MQ, c, :], lambda c, m: m_bsel[0:32, c, 0:m])
                head_norms([(MQ, TJ)] + [(HD, TJ)] * 15, 32, TJ, lambda c: m_sel[0:HD if c else MQ, c, :],
                           lambda c, m: m_bsel[0:32, c, 0:m])
                told()
                for part in range(9):
                    b = small_out()
                    v = (m_q[64:96, 2 * part:2 * part + 2, :] if part < 8 else m_k[64:96, 0:1, 0:T])
                    mm(psum[64:96, b, 0:T * v.shape[1]], rot_m[64:96, :], v, start=True, stop=True).then_inc(small_done, 1)
                told()
                softmax_jobs(list(latent_jobs()))
                out_proj()

            pe.wait_ge(base_loaded, 48)
            told()
            norm(T)
            ffn(0, peel=1)
            norm(T)
            pe.wait_ge(phase_loaded[0], 16)
            hybrid()
            norm(T)
            ffn(1)
            norm(T)
            ffn(2)
            norm(T)
            stick()
            norm(T)
            ffn(3)

            norm(TJ, halves=2)
            even()
            norm(TJ, halves=2)
            pe.wait_ge(h_ready, pos.n("h"))
            mlp_joint()
            mlp_joint()
            norm(TJ, halves=2)
            latent()
            norm(T)
            mlp_latent()


_EVENTS = {"ffn_in0": 1, "ffn_out0": 1, "hy_in": 1, "hy_out": 1, "ffn_in1": 1, "ffn_out1": 1, "ffn_in2": 1,
           "ffn_out2": 1, "sb_in": 1, "sb_out": 1, "ffn_in3": 1, "ffn_out3": 1, "e_in": 2, "e_out": 2}
EV, _e = {}, 0
for _name, _n, _w in weight_plan():
    EV[_name] = _e
    _e += _n * _EVENTS.get(_name, 0)
_UNITS = {"ffn_out0": 8, "ffn_out1": 8, "ffn_out2": 8, "ffn_out3": 8, "e_in": 18, "e_out": 8, "mlp_in0": 16,
          "mlp_in1": 16, "o_in": 6, "o_uq": 8, "o_ukv": 24, "mlp_out2": 8}
FINAL_UNITS = sum(_UNITS.get(name, n) for name, n, _ in weight_plan())
Y_EVEN = 4 + 16


def _cols(a, chunks):
    return np.asarray(a, np.float32).reshape(chunks, P).T


def _panel(w, c0, c1):
    k = w.shape[0] // P
    out = w[:, c0:c1].reshape(k, P, c1 - c0).transpose(1, 0, 2).reshape(P, -1)
    pad = SLOT - out.shape[1]
    return np.pad(out, ((0, 0), (0, pad))) if pad > 0 else out


def _weights(i):
    parts = {}

    def ffn(f):
        w_in, w_out = i["ffn_w_in"][f // 2, f % 2], i["ffn_w_out"][f // 2, f % 2]
        ins = []
        for c in range(FC):
            a, b = (w_in[:, o + c * P:o + (c + 1) * P].reshape(DC, P, P) for o in (0, FF))
            ins.append(np.stack([a, b], axis=1).reshape(DC, 2, P, P).transpose(2, 0, 1, 3).reshape(P, SLOT))
        outs = []
        for c in range(DC):
            w = w_out[:, c * P:(c + 1) * P].reshape(FC, P, P).transpose(1, 0, 2)
            outs += [w[:, 0:FH].reshape(P, -1), w[:, FH:].reshape(P, -1)]
        parts[f"ffn_in{f}"], parts[f"ffn_out{f}"] = ins, outs

    for f in range(4):
        ffn(f)

    def panels(w, n):
        return [_panel(w, 2 * P * k, 2 * P * (k + 1)) for k in range(n)]

    parts["hy_in"] = panels(i["hy_w_in"][0], 10)
    parts["hy_out"] = panels(i["hy_w_out"][0], 4)
    parts["sb_in"] = panels(i["sb_w_qkv"][0], 12)
    parts["sb_out"] = panels(i["sb_w_out"][0], 4)
    parts["e_in"] = panels(i["e_w_in_2"][0], 9)
    parts["e_out"] = panels(i["e_w_out_2"][0], 4)
    w1, w2 = i["mlp_w1_2"], i["mlp_w2_2"]
    for half in range(2):
        parts[f"mlp_in{half}"] = panels(w1[0][:, half * 2048:(half + 1) * 2048], 8)
        parts[f"mlp_out{half}"] = [_panel(w2[0][half * 2048:(half + 1) * 2048], P * c, P * (c + 1)) for c in range(DC)]
    o = i["o_w_in_2"][0]
    parts["o_in"] = [_panel(o, 0, 256), _panel(o, 256, 512), _panel(o, 512, 672)]
    uq = i["o_w_uq_2"][0]
    parts["o_uq"] = [_panel(uq, 0, 576), _panel(uq, 576, 1152), _panel(uq, 1152, 1536)]
    parts["o_ukv"] = [_panel(i["o_w_ukv_2"][0], D * k, D * (k + 1)) for k in range(2)]
    parts["o_out"] = panels(i["o_w_out_2"][0], 4)
    parts["mlp_in2"] = panels(w1[1], 16)
    parts["mlp_out2"] = [_panel(w2[1][half * 2048:(half + 1) * 2048], P * c, P * (c + 1))
                         for c in range(DC) for half in range(2)]
    total = sum(n * P * w for _, n, w in weight_plan())
    flat, at = np.empty(total, np.float32), 0
    for name, n, w in weight_plan():
        assert len(parts[name]) == n, name
        for a in parts[name]:
            assert a.shape == (P, w), (name, a.shape)
            flat[at:at + P * w] = a.reshape(-1)
            at += P * w
    return flat


def _vectors(i):
    v = np.zeros((P, NV), np.float32)

    def put(name, a):
        v[:a.shape[0], VOFF[name]:VOFF[name] + a.shape[1]] = a

    two = lambda a: np.concatenate([a, a])[:, None]
    put("ffn_norm", _cols(i["ffn_norm"].reshape(-1), 32))
    put("mix_norm", _cols(i["mix_norm"].reshape(-1), 16))
    put("conv_w", _cols(i["rg_conv_w"][0].reshape(-1), 16))
    put("conv_b", _cols(i["rg_conv_b"][0], 4))
    put("gate_b", _cols(i["rg_gate_b"][0].reshape(-1), 8))
    put("lam", _cols(i["rg_lambda"][0], 4))
    put("fox_g", np.concatenate([two(i["fox_qk_norm"][0, 0]), two(i["fox_qk_norm"][0, 1])], axis=1))
    put("fox_fb", i["fox_fgate_b"][0][:, None])
    put("norm_mix", _cols(i["norm_mix_2"].reshape(-1), 16))
    put("norm_mlp", _cols(i["norm_mlp_2"].reshape(-1), 16))
    for name in ("a_qn", "a_kn", "b_qn", "b_kn"):
        put(name, two(i[{"a_qn": "a_q_norm_2", "a_kn": "a_k_norm_2", "b_qn": "b_q_norm_2", "b_kn": "b_k_norm_2"}[name]][0]))
    put("qa_norm", _cols(i["o_qa_norm_2"][0], 3))
    put("kva_norm", _cols(i["o_kva_norm_2"][0], 2))
    put("qn", np.concatenate([i["o_qn_nope_2"][0], i["o_qn_rope_2"][0]])[:, None])
    put("kn", np.concatenate([i["o_kn_nope_2"][0], i["o_kn_rope_2"][0]])[:, None])
    put("ada_b", _cols(i["ada_b_2"].reshape(-1), 96))
    cond = np.stack([i["c_2"][0], i["c_ctx_2"]], axis=-1)
    put("cond", cond.reshape(DC, P, 2).transpose(1, 0, 2).reshape(P, 16))
    put("sink", np.broadcast_to(i["a_sink_2"][0], (P, 8)))
    return v


def _rope(rows, half):
    t = np.arange(T)
    inv = (np.float32(10000.0) ** (-np.arange(half, dtype=np.float32) / np.float32(half))).astype(np.float32)
    cos, sin, rot = np.zeros((rows, T), np.float32), np.zeros((rows, T), np.float32), np.zeros((rows, rows), np.float32)
    for r in range(rows):
        e = r % (2 * half)
        where = (t // GRID if (r // (2 * half)) % 2 == 0 else t % GRID).astype(np.float32)
        angle = where * inv[e % half]
        cos[r], sin[r] = np.cos(angle), np.sin(angle)
        if e < half:
            rot[r + half, r] = -1.0
        else:
            rot[r - half, r] = 1.0
    return cos, sin, rot


def _join(*parts):
    out = []
    for a in parts:
        a = np.asarray(a, np.float32).reshape(a.shape[0], -1)
        out.append(np.pad(a, ((0, P - a.shape[0]), (0, 0))))
    return np.ascontiguousarray(np.concatenate(out, axis=1))


def _head_tables(chunks, width):
    sel, bsel = np.zeros((P, chunks, width), np.float32), np.zeros((width, chunks, P), np.float32)
    for c in range(chunks):
        for half in range(2):
            sel[64 * half:64 * half + 64, c, 2 * c + half] = 1.0 / HD
            bsel[2 * c + half, c, 64 * half:64 * half + 64] = 1.0
    return sel, bsel


def _arrays(i):
    q, k = np.arange(T)[:, None], np.arange(T)[None, :]
    by_tile = lambda m: np.where(m, 0.0, NEG).astype(np.float32).reshape(2, P, T).transpose(1, 0, 2)
    out = {"weights": _weights(i), "vecs": _vectors(i)}
    out["ada"] = np.stack([_panel(i["ada_w_2"][layer], 2 * P * k, 2 * P * (k + 1))
                           for layer in range(2) for k in range(24)])
    both = np.concatenate([i["x"][0], i["ctx_2"][0]], axis=0)
    out["x"] = np.ascontiguousarray(both.T.reshape(DC, P, TJ).transpose(1, 0, 2))
    out["base_c"] = _join(np.eye(P), np.full((P, P), 1.0 / D))
    sel, bsel = _head_tables(8, 16)
    eh = np.zeros((8, 8, P), np.float32)
    for h in range(8):
        eh[h, h] = 1.0
    gwm = np.zeros((P, 2, 4, P), np.float32)
    for g in range(2):
        for h in range(8):
            r = 64 * (h % 2)
            gwm[r:r + 64, g, h // 2, r:r + 64] = i["rg_gate_w"][0, g, h]
    wf = i["hy_w_in"][0][:, 2560:2568].reshape(DC, P, 8).transpose(1, 0, 2)
    out["fox_c"] = _join(by_tile(k <= q), sel, bsel, eh, gwm, wf)
    kp, qq = np.arange(P)[:, None], np.arange(T)[None, :]
    m0 = np.where(kp < qq, 0.0, NEG)
    m1 = np.where(kp + P < qq[:, P:], 0.0, NEG)
    tri = np.where(np.arange(P)[:, None] >= np.arange(P)[None, :], -1.0, 0.0)
    out["sb_c"] = _join(np.concatenate([m0, m1], axis=1), tri, -np.ones((P, P)))
    sel, bsel = _head_tables(13, 32)
    cos, sin, rot = _rope(P, 16)
    out["even_c"] = _join(sel, bsel, cos, sin, rot)
    cq = np.arange(GRID)
    c0 = np.clip(cq - NA_COLS // 2, 0, GRID - NA_COLS)
    ok = (cq[None, :] >= c0[:, None]) & (cq[None, :] < c0[:, None] + NA_COLS)
    out["even_m"] = _join(by_tile(np.abs(q - k) <= 128), np.tile(np.where(ok, 0.0, NEG), (2, 4)))
    pad = np.pad(i["b_rpb_2"][0], ((0, 0), (0, 0), (GRID - NA_COLS, GRID - NA_COLS)))
    r, c = (a.reshape(2, P).T[:, :, None] for a in (np.arange(T) // GRID, np.arange(T) % GRID))
    kr, kc = np.arange(T) // GRID, np.arange(T) % GRID
    rel = pad[:, kr - r + 7, kc - c + GRID - 1]
    out["rpb"] = np.ascontiguousarray(rel.transpose(1, 2, 0, 3).reshape(P, -1))
    sel, bsel = np.zeros((MQ, 16, 32), np.float32), np.zeros((32, 16, MQ), np.float32)
    for h in range(16):
        sel[0:HD, h, 2 * h], sel[HD:, h, 2 * h + 1] = 1.0 / HD, 1.0 / MR
        bsel[2 * h, h, 0:HD] = bsel[2 * h + 1, h, HD:] = 1.0
    cos, sin, rot = (np.concatenate([np.zeros((64, a.shape[1]), np.float32), a]) for a in _rope(MR, 8))
    out["latent_c"] = _join(sel, bsel, cos, sin, rot)
    return out


def kernel(**inputs):
    import concourse.bacc as bacc
    from concourse.bass_utils import run_bass_kernel_spmd

    arrays = _arrays({k: np.asarray(v) for k, v in inputs.items()})
    nc = bacc.Bacc("TRN2", target_bir_lowering=False, num_devices=1)
    ap = {name: nc.dram_tensor(f"in_{name}", a.shape, mybir.dt.from_np(a.dtype), kind="ExternalInput").ap()
          for name, a in arrays.items()}
    ap["out"] = nc.dram_tensor("out_x", (P, DC, T), F32, kind="ExternalOutput").ap()
    build(nc, ap)
    r = run_bass_kernel_spmd(nc, [{f"in_{name}": a for name, a in arrays.items()}], core_ids=[0])
    y = np.asarray(r.results[0]["out_x"])
    return np.ascontiguousarray(y.transpose(1, 0, 2).reshape(D, T).T.reshape(1, T, D))
```
